# Optimizing a Trainium2 kernel written in Bass

```python
import jax, jax.numpy as jnp
from jax import lax
import numpy as np

D_MODEL = 2048
BATCH = 1
SEQ = 256
DEPTH = 2
DEC_BATCH = 8
DEC_SEQ = 8
PAST_LEN = 2048
PAGE_SIZE = 128

N_A_LAYERS = DEPTH // 2
N_B_LAYERS = DEPTH - N_A_LAYERS
CONV_A_WIDTH = 31
FFN_CONV_WIDTH = 3
D_FF = ((8 * D_MODEL // 3 + 255) // 256) * 256
HEAD_DIM = 64
N_HEADS = D_MODEL // HEAD_DIM
N_KV_HEADS = max(1, N_HEADS // 8)
GROUP = N_HEADS // N_KV_HEADS
WINDOW = 128
BLOCK = WINDOW
DN_ALPHA = (2.0 * DEPTH) ** 0.25
DN_BETA = (8.0 * DEPTH) ** -0.25
LN_EPS = 1e-5
NEG_BIG = -1e30

kernel_name = 'yoco_conformer_swa_sink_decoder_step'

def layer_norm(x, g, b):
    xf = x.astype(jnp.float32)
    mu = jnp.mean(xf, axis=-1, keepdims=True)
    var = jnp.mean(jnp.square(xf - mu), axis=-1, keepdims=True)
    y = (xf - mu) * lax.rsqrt(var + LN_EPS) * g.astype(jnp.float32) + b.astype(jnp.float32)
    return y.astype(x.dtype)

def causal_dwconv(u, prev, w, bias):
    ext = jnp.concatenate([prev.astype(u.dtype), u], axis=1)
    y = lax.conv_general_dilated(ext, w[:, None, :].astype(u.dtype), window_strides=(1,), padding='VALID',
                                 dimension_numbers=('NWC', 'WIO', 'NWC'), feature_group_count=u.shape[-1])
    return y + bias, ext[:, -(w.shape[0] - 1):]

def conformer_conv(x, prev, w_in, b_in, w_dw, b_dw, g_n, b_n, w_out, b_out):
    a, gate = jnp.split(x @ w_in + b_in, 2, axis=-1)
    u = a * jax.nn.sigmoid(gate)
    u, new_prev = causal_dwconv(u, prev, w_dw, b_dw)
    u = jax.nn.silu(layer_norm(u, g_n, b_n))
    return u @ w_out + b_out, new_prev

def conv_ffn(x, prev, w_up, w_dw, b_dw, w_down):
    g, v = jnp.split(x @ w_up, 2, axis=-1)
    g, new_prev = causal_dwconv(g, prev, w_dw, b_dw)
    return (jax.nn.gelu(g, approximate=False) * v) @ w_down, new_prev

def alibi_slopes():
    return 2.0 ** (-8.0 * jnp.arange(1, N_HEADS + 1, dtype=jnp.float32) / N_HEADS)

def _band(a, nb):
    a = a.reshape((a.shape[0], nb + 1, BLOCK) + a.shape[2:])
    return jnp.concatenate([a[:, :-1], a[:, 1:]], axis=2)

def sink_window_attention(q, k_ext, v_ext, key_valid, sinks):
    n, t = q.shape[:2]
    if t % BLOCK == 0:
        nb, qb = t // BLOCK, BLOCK
        kb, vb = _band(k_ext, nb), _band(v_ext, nb)
        valid = _band(key_valid[None], nb)[0]
    else:
        nb, qb = 1, t
        kb, vb = k_ext[:, None], v_ext[:, None]
        valid = key_valid[None]
    qg = q.reshape(n, nb, qb, N_KV_HEADS, GROUP, HEAD_DIM)
    s = jnp.einsum('nbqkgd,nbskd->nbkgqs', qg, kb, preferred_element_type=jnp.float32) * (HEAD_DIM ** -0.5)
    dist = WINDOW + jnp.arange(qb)[:, None] - jnp.arange(kb.shape[2])[None, :]
    slopes = alibi_slopes().reshape(N_KV_HEADS, GROUP)[:, :, None, None]
    s = s - slopes * dist.astype(jnp.float32)
    mask = ((dist >= 0) & (dist <= WINDOW))[None] & valid[:, None, :]
    s = jnp.where(mask[:, None, None], s, NEG_BIG)
    sink = sinks.astype(jnp.float32).reshape(N_KV_HEADS, GROUP)[:, :, None, None]
    m = jnp.maximum(jnp.max(s, axis=-1, keepdims=True), sink)
    p = jnp.exp(s - m)
    p = (p / (jnp.sum(p, axis=-1, keepdims=True) + jnp.exp(sink - m))).astype(v_ext.dtype)
    o = jnp.einsum('nbkgqs,nbskd->nbqkgd', p, vb)
    return o.reshape(n, t, N_HEADS * HEAD_DIM)

def trunk(x, conv_a_prev, ffn_prev, k_prev, v_prev, prev_valid, params):
    (a_w_in, a_b_in, a_w_dw, a_b_dw, a_norm_g, a_norm_b, a_w_out, a_b_out, w_kv, b_w_q, b_sinks, b_w_o,
     f_w_up, f_w_dw, f_b_dw, f_w_down, ln_mix_g, ln_mix_b, ln_ffn_g, ln_ffn_b) = params
    n, t = x.shape[:2]
    new_conv_a, new_ffn = [], []
    k_ext = v_ext = key_valid = None
    for l in range(DEPTH):
        if l < N_A_LAYERS:
            mix, st = conformer_conv(x, conv_a_prev[l], a_w_in[l], a_b_in[l], a_w_dw[l], a_b_dw[l],
                                     a_norm_g[l], a_norm_b[l], a_w_out[l], a_b_out[l])
            new_conv_a.append(st)
        else:
            j = l - N_A_LAYERS
            q = (x @ b_w_q[j]).reshape(n, t, N_HEADS, HEAD_DIM)
            mix = sink_window_attention(q, k_ext, v_ext, key_valid, b_sinks[j]) @ b_w_o[j]
        x = layer_norm(DN_ALPHA * x + mix, ln_mix_g[l], ln_mix_b[l])
        f, st = conv_ffn(x, ffn_prev[l], f_w_up[l], f_w_dw[l], f_b_dw[l], f_w_down[l])
        new_ffn.append(st)
        x = layer_norm(DN_ALPHA * x + f, ln_ffn_g[l], ln_ffn_b[l])
        if l == N_A_LAYERS - 1:
            kv = (x @ w_kv).reshape(n, t, 2, N_KV_HEADS, HEAD_DIM)
            k_ext = jnp.concatenate([k_prev.astype(x.dtype), kv[:, :, 0]], axis=1)
            v_ext = jnp.concatenate([v_prev.astype(x.dtype), kv[:, :, 1]], axis=1)
            key_valid = jnp.concatenate([jnp.full((WINDOW,), prev_valid), jnp.ones((t,), dtype=bool)])
    return x, jnp.stack(new_conv_a), jnp.stack(new_ffn), k_ext[:, -WINDOW:], v_ext[:, -WINDOW:]

def setup_inputs(seed: int = 0) -> dict:
    key = jax.random.key(seed)
    ks = jax.random.split(key, 32)
    nrm = lambda k, shape, scale: jax.random.normal(k, shape, dtype=jnp.float32) * scale
    D, F, KVW = D_MODEL, D_FF, N_KV_HEADS * HEAD_DIM
    return {
        'x_prompt': nrm(ks[0], (BATCH, SEQ, D), 1.0),
        'x_sample': nrm(ks[1], (DEC_BATCH, DEC_SEQ, D), 1.0),
        'state_conv_a': nrm(ks[2], (N_A_LAYERS, DEC_BATCH, CONV_A_WIDTH - 1, D), 0.5),
        'state_ffn_conv': nrm(ks[3], (DEPTH, DEC_BATCH, FFN_CONV_WIDTH - 1, F), 1.0),
        'cache_k_win': nrm(ks[4], (DEC_BATCH, WINDOW, N_KV_HEADS, HEAD_DIM), 1.0),
        'cache_v_win': nrm(ks[5], (DEC_BATCH, WINDOW, N_KV_HEADS, HEAD_DIM), 1.0),
        'a_w_in': nrm(ks[6], (N_A_LAYERS, D, 2 * D), D ** -0.5),
        'a_b_in': nrm(ks[7], (N_A_LAYERS, 2 * D), 0.02),
        'a_w_dw': nrm(ks[8], (N_A_LAYERS, CONV_A_WIDTH, D), CONV_A_WIDTH ** -0.5),
        'a_b_dw': nrm(ks[9], (N_A_LAYERS, D), 0.02),
        'a_norm_g': 1.0 + nrm(ks[10], (N_A_LAYERS, D), 0.02),
        'a_norm_b': nrm(ks[11], (N_A_LAYERS, D), 0.02),
        'a_w_out': nrm(ks[12], (N_A_LAYERS, D, D), D ** -0.5 * DN_BETA),
        'a_b_out': nrm(ks[13], (N_A_LAYERS, D), 0.02),
        'w_kv': nrm(ks[14], (D, 2 * KVW), D ** -0.5),
        'b_w_q': nrm(ks[15], (N_B_LAYERS, D, N_HEADS * HEAD_DIM), D ** -0.5),
        'b_sinks': nrm(ks[16], (N_B_LAYERS, N_HEADS), 0.5),
        'b_w_o': nrm(ks[17], (N_B_LAYERS, N_HEADS * HEAD_DIM, D), (N_HEADS * HEAD_DIM) ** -0.5 * DN_BETA),
        'f_w_up': nrm(ks[18], (DEPTH, D, 2 * F), D ** -0.5),
        'f_w_dw': nrm(ks[19], (DEPTH, FFN_CONV_WIDTH, F), FFN_CONV_WIDTH ** -0.5),
        'f_b_dw': nrm(ks[20], (DEPTH, F), 0.02),
        'f_w_down': nrm(ks[21], (DEPTH, F, D), F ** -0.5 * DN_BETA),
        'ln_mix_g': 1.0 + nrm(ks[22], (DEPTH, D), 0.02),
        'ln_mix_b': nrm(ks[23], (DEPTH, D), 0.02),
        'ln_ffn_g': 1.0 + nrm(ks[24], (DEPTH, D), 0.02),
        'ln_ffn_b': nrm(ks[25], (DEPTH, D), 0.02),
    }

def reference(x_prompt, x_sample, state_conv_a, state_ffn_conv, cache_k_win, cache_v_win,
              a_w_in, a_b_in, a_w_dw, a_b_dw, a_norm_g, a_norm_b, a_w_out, a_b_out,
              w_kv, b_w_q, b_sinks, b_w_o, f_w_up, f_w_dw, f_b_dw, f_w_down,
              ln_mix_g, ln_mix_b, ln_ffn_g, ln_ffn_b):
    params = (a_w_in, a_b_in, a_w_dw, a_b_dw, a_norm_g, a_norm_b, a_w_out, a_b_out, w_kv, b_w_q, b_sinks, b_w_o,
              f_w_up, f_w_dw, f_b_dw, f_w_down, ln_mix_g, ln_mix_b, ln_ffn_g, ln_ffn_b)
    bp, dt = x_prompt.shape[0], x_prompt.dtype
    zero_conv_a = jnp.zeros((N_A_LAYERS, bp, CONV_A_WIDTH - 1, D_MODEL), dt)
    zero_ffn = jnp.zeros((DEPTH, bp, FFN_CONV_WIDTH - 1, D_FF), dt)
    zero_kv = jnp.zeros((bp, WINDOW, N_KV_HEADS, HEAD_DIM), dt)
    y_prompt, conv_a_prompt, ffn_conv_prompt, k_win_prompt, v_win_prompt = trunk(
        x_prompt, zero_conv_a, zero_ffn, zero_kv, zero_kv, False, params)
    y_sample, conv_a_sample, ffn_conv_sample, k_win_sample, v_win_sample = trunk(
        x_sample, state_conv_a, state_ffn_conv, cache_k_win, cache_v_win, True, params)
    return (y_prompt, y_sample, conv_a_prompt, ffn_conv_prompt, k_win_prompt, v_win_prompt,
            conv_a_sample, ffn_conv_sample, k_win_sample, v_win_sample)


_drawn_inputs = setup_inputs


def setup_inputs(seed=0):
    import zlib

    import numpy as np

    out = dict(_drawn_inputs(seed))
    spreads = {}
    factors = {'a_b_dw': 5.772,
     'a_norm_g': 8.0,
     'a_norm_b': 8.0,
     'a_b_out': 3.623,
     'b_sinks': 4.59,
     'f_b_dw': 8.0}
    for name, (base, spread) in spreads.items():
        noise = np.random.default_rng([zlib.crc32(name.encode()), seed]).standard_normal(out[name].shape)
        drawn = base * np.exp(spread * noise) if base else spread * noise
        out[name] = __import__('jax').numpy.asarray(drawn.astype(out[name].dtype))
    for name, factor in factors.items():
        out[name] = (out[name] * factor).astype(out[name].dtype)
    return out
```

```python
from contextlib import ExitStack, nullcontext
from collections import namedtuple

import numpy as np

import concourse.bass as bass
from concourse import mybir

F32 = mybir.dt.float32
F32R = mybir.dt.float32r
ALU = mybir.AluOpType
ACT = mybir.ActivationFunctionType
AXX = mybir.AxisListType.X

P = 128
D = 2048
KD = D // P
SEQ = 256
NB, NQ = 8, 8
NS = NB * NQ
T = SEQ + NS
DFF = 5632
KF = DFF // P
HALF = KF // 2
LAYERS = 2
CW = 31
HIST = CW - 1
FW = 3
SEG = 8
NSEG = T // SEG
PSEG = SEQ // SEG
SEGW = HIST + SEG
HD = 64
NH = 32
WINDOW = 128
SKEYS = WINDOW + NQ
ALPHA = float((2.0 * LAYERS) ** 0.25)
EPS = 1e-5
QSCALE = float(HD ** -0.5)
MASKED = 1e35

Phase = namedtuple("Phase", "name base groups kt")


def phases():
    out, base = {}, 0
    order = [("w_in", 2 * KD, 8), ("w_out", KD, 8)]
    for l in range(LAYERS):
        if l == 1:
            order += [("w_kv", 4, 8), ("w_q", KD, 8), ("w_o", KD, 8)]
        for h in range(2):
            order += [(f"up{l}{h}", 2 * HALF, 8), (f"down{l}{h}", KD, HALF // 2)]
    for name, groups, kt in order:
        out[name] = Phase(name, base, groups, kt)
        base += groups
    return out


PARAMS = [("b_in", (2 * KD, 1)), ("w_dw", (KD, CW)), ("b_dw", (KD, 1)), ("norm_g", (KD, 1)), ("norm_b", (KD, 1)),
          ("b_out", (KD, 1)), ("f_w_dw", (LAYERS * KF, FW)), ("f_b_dw", (LAYERS * KF, 1)),
          ("mix_g", (LAYERS * KD, 1)), ("mix_b", (LAYERS * KD, 1)), ("ffn_g", (LAYERS * KD, 1)),
          ("ffn_b", (LAYERS * KD, 1)), ("sinks", (NH, 1)), ("sinks_s", (2, 1))]
CONSTS = [("ident", (P,)), ("ones_mean", (P,)), ("dist", (3, P)), ("dist_s", (SKEYS,)),
          ("negslope", (NH, 1)), ("negslope_s", (2, 1)), ("eps", (1,))]


def columns(table):
    at, out = 0, {}
    for name, shape in table:
        n = int(np.prod(shape))
        out[name] = (at, n, shape)
        at += n
    return out, at


def trunk_kernel(nc, io):
    ph = phases()
    pcols, n_params = columns(PARAMS)
    ccols, n_consts = columns(CONSTS)

    with ExitStack() as ctx:
        def sb(name, shape, dt=F32):
            return ctx.enter_context(nc.sbuf_tensor(name, shape, dt))

        def sem(name):
            return ctx.enter_context(nc.semaphore(name))

        def bank(name):
            return ctx.enter_context(nc.psum_tensor(name, [P, 512], F32))

        xr = sb("xr", [P, KD, T])
        xh = sb("xh", [P, KD, T], F32R)
        xl = sb("xl", [P, KD, T], F32R)
        CHUNK = HALF // 2 * P
        w_raw = sb("w_raw", [P, 4, CHUNK])
        w_hi = sb("w_hi", [P, 4, CHUNK], F32R)
        w_lo = sb("w_lo", [P, 4, CHUNK], F32R)
        params = sb("params", [P, n_params])
        consts = sb("consts", [P, n_consts])
        work = sb("work", [P, 2, T])
        rstd = sb("rstd", [P, T])
        acc_sum = sb("acc_sum", [P, T])
        ffn_in = sb("ffn_in", [P, KF, NB, FW - 1])
        ffn_out = sb("ffn_out", [P, KF, NB + 1, FW - 1])
        gate_s = sb("gate_s", [P, NB, FW - 1 + NQ])
        with nc.sbuf_tensor("conv_y", [P, KD, T], F32) as conv_y, \
                nc.sbuf_tensor("u_pad", [P, HIST + T], F32) as u_pad, \
                nc.sbuf_tensor("u_seg", [P, NSEG, SEGW], F32) as u_seg, \
                nc.sbuf_tensor("taps_odd", [P, T], F32) as taps_odd:
            pass
        with nc.sbuf_tensor("k_t", [P, 2, T], F32) as k_t, \
                nc.sbuf_tensor("kc_t", [P, 2, NB, WINDOW], F32) as kc_t, \
                nc.sbuf_tensor("v_c", [P, NB, 4 * HD], F32) as v_c, \
                nc.sbuf_tensor("v_p", [P, 2, 4 * HD], F32) as v_p, \
                nc.sbuf_tensor("v_n", [P, NB, 4 * HD], F32) as v_n, \
                nc.sbuf_tensor("qo", [P, KD, T], F32) as qo, \
                nc.sbuf_tensor("q_st", [P, 2, SEQ], F32) as q_st, \
                nc.sbuf_tensor("q_s", [P, 2, NB, 8, NQ], F32) as q_s, \
                nc.sbuf_tensor("probs", [P, 2, 3, P], F32) as probs, \
                nc.sbuf_tensor("probs_t", [P, 6 * P], F32) as probs_t, \
                nc.sbuf_tensor("smx", [P, 6, 6], F32) as smx:
            pass
        hh = sb("hh", [P, HALF, T], F32R)
        hl = sb("hl", [P, HALF, T], F32R)

        acc = [bank("acc0"), bank("acc1")]
        sc = [bank("sc0"), bank("sc1")]
        pt = [bank("pt0"), bank("pt1")]
        ot = bank("ot")
        st = bank("st")

        def par(name):
            a, n, shape = pcols[name]
            return params[:, a:a + n].rearrange("p (i t) -> p i t", t=shape[1])

        def const(name):
            a, n, shape = ccols[name]
            v = consts[:, a:a + n]
            return v.rearrange("p (i t) -> p i t", t=shape[1]) if len(shape) == 2 else v

        ident, ones_mean = const("ident"), const("ones_mean")
        v_t = work[:, :, :]
        probs_s = probs[:, :, :, :].rearrange("p a b c -> p (a b c)")[:, 0:4 * SKEYS].rearrange(
            "p (u k) -> p u k", u=4)
        probs_tn = work[:, :, :].rearrange("p a b -> p (a b)")
        rowmax, negmax = smx[:, 0, :], smx[:, 1, 0:4]
        rowsum, sinkexp = smx[:, 2, 0:4], smx[:, 3, 0:4]
        denom, rdenom = smx[:, 4, 0:4], smx[:, 5, 0:4]

        raw_loaded = [sem(f"raw_loaded{s}") for s in range(4)]
        hi_ready, lo_ready = sem("hi_ready"), sem("lo_ready")
        multiplied = sem("multiplied")
        bank_read = [sem("bank_read0"), sem("bank_read1")]
        x_loaded = [sem(f"x_loaded{q}") for q in range(4)]
        tables_loaded = sem("tables_loaded")
        rhs_hi_ready, rhs_ready = sem("rhs_hi_ready"), sem("rhs_ready")
        zero_ready = sem("zero_ready")
        state_loaded, state_saved, useg_built = sem("state_loaded"), sem("state_saved"), sem("useg_built")
        conv_step = sem("conv_step")
        mean_ready, centered, squared = sem("mean_ready"), sem("centered"), sem("squared")
        var_added, std_ready = sem("var_added"), sem("std_ready")
        rstd_ready, scaled = sem("rstd_ready"), sem("scaled")
        sum_added = sem("sum_added")
        ffn_in_loaded, ffn_out_saved = sem("ffn_in_loaded"), sem("ffn_out_saved")
        gate_taken, taps_done, gelu_done = sem("gate_taken"), sem("taps_done"), sem("gelu_done")
        h_hi_ready, h_ready = sem("h_hi_ready"), sem("h_ready")
        cache_loaded, kv_saved = sem("cache_loaded"), sem("kv_saved")
        v_transposed, v_taken = sem("v_transposed"), sem("v_taken")
        scores_ready, scores_read, softmax_step = sem("scores_ready"), sem("scores_read"), sem("softmax_step")
        exp_done, probs_turned, probs_taken = sem("exp_done"), sem("probs_turned"), sem("probs_taken")
        out_ready, out_read = sem("out_ready"), sem("out_read")
        s_scores_ready, s_scores_read, s_step = sem("s_scores_ready"), sem("s_scores_read"), sem("s_step")
        s_exp_done, s_turned, s_taken = sem("s_exp_done"), sem("s_turned"), sem("s_taken")
        s_out_ready, s_out_read = sem("s_out_ready"), sem("s_out_read")
        y_ready, y_saved = sem("y_ready"), sem("y_saved")

        def chunk(p, ip, par_, j):
            return 2 * p.base + 4 * ip + 2 * par_ + j

        def group_done(p, ip, par_):
            return chunk(p, ip, par_, 0) + 2

        def bank_count(p, ip):
            return p.base // 2 + ip + 1

        RHS_X, RHS_CONV, RHS_MIX0, RHS_FFN0, RHS_ATTN, RHS_MIX1 = (KD * e for e in range(6))
        order = list(ph.values())
        after = {a.name: b for a, b in zip(order, order[1:])}

        block = ctx.enter_context(nc.Block())

        @block.sync
        def _(sp):
            def load(p, ip, par_, wait=True):
                for j in range(2):
                    slot, n = 2 * par_ + j, p.kt * P
                    if wait:
                        sp.wait_ge(lo_ready, chunk(p, ip, par_, j) - 3)
                    sp.dma_start(w_raw[:, slot, 0:n], io[p.name][2 * ip + par_, :, j * n:(j + 1) * n]
                                 ).then_inc(raw_loaded[slot], 16)

            for p in order:
                first = 0
                if p.base == 0:
                    first = 1
                    load(p, 0, 0, wait=False)
                    load(p, 0, 1, wait=False)
                with sp.Fori(first, p.groups // 2) as ip:
                    load(p, ip, 0)
                    load(p, ip, 1)
            for q in range(4):
                sp.wait_ge(y_ready, 4 * (q + 1))
                sp.dma_start(io["y"][:, 4 * q:4 * q + 4, :], xr[:, 4 * q:4 * q + 4, :]).then_inc(y_saved, 16)
            sp.wait_ge(y_saved, 64)

        @block.gpsimd
        def _(pool):
            pool.dma_start(params[:, :], io["params"]).then_inc(tables_loaded, 16)
            pool.dma_start(consts[:, :], io["consts"]).then_inc(tables_loaded, 16)
            pool.dma_start(u_seg[:, PSEG:NSEG, 0:HIST], io["conv_state"][:, 0]).then_inc(state_loaded, 16)
            pool.dma_start(ffn_in[:, :, :, :], io["ffn_state"][0]).then_inc(ffn_in_loaded, 16)
            pool.dma_start(io["kc_out"], io["k_cache"][:, NQ:WINDOW, :]).then_inc(kv_saved, 16)
            pool.dma_start(io["vc_out"], io["v_cache"][:, NQ:WINDOW, :]).then_inc(kv_saved, 16)

            def save_conv_state(i):
                pool.wait_ge(useg_built, i + 1)
                pool.wait_ge(state_loaded, 16 * i + 16)
                pool.dma_start(io["conv_state_out"][:, i], u_seg[:, PSEG - 1:NSEG, SEG:SEGW]).then_inc(state_saved, 16)

            with pool.Fori(0, KD - 1) as i:
                save_conv_state(i)
                pool.wait_ge(conv_step, 32 * i + 32)
                pool.wait_ge(state_saved, 16 * i + 16)
                pool.dma_start(u_seg[:, PSEG:NSEG, 0:HIST], io["conv_state"][:, i + 1]).then_inc(state_loaded, 16)
            save_conv_state(KD - 1)

            pool.wait_ge(h_ready, KF)
            pool.dma_start(io["ffn_state_out"][0], ffn_out[:, :, :, :]).then_inc(ffn_out_saved, 16)
            pool.dma_start(ffn_in[:, :, :, :], io["ffn_state"][1]).then_inc(ffn_in_loaded, 16)
            pool.wait_ge(multiplied, 2 * ph["w_kv"].base)
            pool.dma_start(kc_t[:, :, :, :], io["k_cache_t"]).then_inc(cache_loaded, 16)
            pool.dma_start(v_c[:, :, :], io["v_cache"].rearrange("n k c -> k n c")).then_inc(cache_loaded, 16)
            pool.wait_ge(bank_read[0], bank_count(ph["w_kv"], 1))
            pool.wait_ge(bank_read[1], bank_count(ph["w_kv"], 1))
            pool.dma_start(io["k_new"], k_t[:, :, :]).then_inc(kv_saved, 16)
            pool.dma_start(io["v_new"], v_t).then_inc(kv_saved, 16)
            pool.wait_ge(h_ready, 2 * KF)
            pool.dma_start(io["ffn_state_out"][1], ffn_out[:, :, :, :]).then_inc(ffn_out_saved, 16)
            pool.wait_ge(state_saved, 16 * KD)
            pool.wait_ge(kv_saved, 64)
            pool.wait_ge(ffn_out_saved, 32)

        @block.tensor
        def _(pe):
            def project_chunk(p, ip, par_, j, hi, lo, rhs_wait=None):
                slot = 2 * par_ + j
                if j == 0 and not (p.base == 0 and isinstance(ip, int) and ip == 0):
                    pe.wait_ge(bank_read[par_], bank_count(p, ip) - 1)
                pe.wait_ge(lo_ready, chunk(p, ip, par_, j) + 1)
                for i in range(p.kt):
                    k = j * p.kt + i
                    if rhs_wait is not None:
                        pe.wait_ge(rhs_wait[0], rhs_wait[1] + k + 1)
                    wh, wl = w_hi[:, slot, i * P:(i + 1) * P], w_lo[:, slot, i * P:(i + 1) * P]
                    out = acc[par_][:, 0:T]
                    first, last = k == 0, k == 2 * p.kt - 1
                    pe.matmul(out, wh, hi[:, k, :], start=first, stop=False)
                    pe.matmul(out, wh, lo[:, k, :], start=False, stop=False)
                    mm = pe.matmul(out, wl, hi[:, k, :], start=False, stop=last)
                mm.then_inc(multiplied, 1)

            def project_group(p, ip, par_, hi, lo, rhs_wait=None):
                for j in range(2):
                    project_chunk(p, ip, par_, j, hi, lo, rhs_wait)

            def project(p, hi, lo, rhs_wait):
                project_group(p, 0, 0, hi, lo, rhs_wait)
                project_group(p, 0, 1, hi, lo)
                with pe.Fori(1, p.groups // 2) as ip:
                    project_group(p, ip, 0, hi, lo)
                    project_group(p, ip, 1, hi, lo)

            def norm_mean(n):
                pe.wait_ge(sum_added, (KD - 1) * n)
                pe.matmul(st[:, 0:T], ones_mean, acc_sum[:, :], start=True, stop=True).then_inc(mean_ready, 1)

            def norm_var(n):
                for k in range(KD):
                    pe.wait_ge(squared, KD * n + k + 1)
                    pe.matmul(ot[:, 0:T], ones_mean, work[:, k % 2, :], start=(k == 0), stop=(k == KD - 1)
                              ).then_inc(var_added, 1)

            p = ph["w_in"]
            pe.wait_ge(tables_loaded, 32)

            def add_conv_sum(i):
                pe.wait_ge(conv_step, 32 * i + 32)
                first, last = isinstance(i, int) and i == 0, isinstance(i, int) and i == KD - 1
                return pe.matmul(st[:, 0:T], ones_mean, conv_y[:, i, :], start=first, stop=last)

            project_group(p, 0, 0, xh, xl, (rhs_ready, RHS_X))
            project_group(p, 0, 1, xh, xl)
            for ip in range(1, 3):
                project_group(p, ip, 0, xh, xl)
                project_group(p, ip, 1, xh, xl)
            add_conv_sum(0)
            with pe.Fori(3, KD) as ip:
                project_group(p, ip, 0, xh, xl)
                project_group(p, ip, 1, xh, xl)
                add_conv_sum(ip - 2)
            add_conv_sum(KD - 2)
            add_conv_sum(KD - 1).then_inc(mean_ready, 1)
            norm_var(0)
            project(ph["w_out"], xh, xl, (rhs_ready, RHS_CONV))
            norm_mean(1)
            norm_var(1)

            def ffn(l, first_rhs):
                for h in range(2):
                    up, down = ph[f"up{l}{h}"], ph[f"down{l}{h}"]
                    project(up, xh, xl, (rhs_ready, first_rhs))
                    project(down, hh, hl, (h_ready, KF * l + HALF * h))

            ffn(0, RHS_MIX0)
            norm_mean(2)
            norm_var(2)

            p = ph["w_kv"]
            project_group(p, 0, 0, xh, xl, (rhs_ready, RHS_FFN0))
            project_group(p, 0, 1, xh, xl)
            project_group(p, 1, 0, xh, xl)
            project_group(p, 1, 1, xh, xl)

            p = ph["w_q"]

            def turn_v():
                pe.wait_ge(bank_read[0], bank_count(ph["w_kv"], 1))
                pe.wait_ge(bank_read[1], bank_count(ph["w_kv"], 1))
                for b in range(2):
                    for a in range(2):
                        pe.transpose(pt[0][:, b * 256 + a * P:b * 256 + (a + 1) * P],
                                     v_t[:, a, b * P:(b + 1) * P], ident)
                for n in range(NB):
                    dst = [sc[0], sc[1], pt[1], ot][n // 2]
                    for a in range(2):
                        tr = pe.transpose(dst[0:NQ, (n % 2) * 256 + a * P:(n % 2) * 256 + (a + 1) * P],
                                          v_t[:, a, SEQ + n * NQ:SEQ + (n + 1) * NQ], ident)
                tr.then_inc(v_transposed, 1)

            def scores(pair, par_, a, first=False):
                t = 2 * pair + par_
                pe.wait_ge(bank_read[par_], bank_count(p, pair))
                if first:
                    pe.wait_ge(v_taken, 1)
                else:
                    pe.wait_ge(scores_read, 2 * t)
                for r in range(2):
                    rows = slice(HD * r, HD * r + HD)
                    pe.matmul(sc[r][:, 0:P], q_st[rows, par_, 0:P], k_t[rows, a, 0:P], start=True, stop=True)
                    pe.matmul(sc[r][:, P:3 * P], q_st[rows, par_, P:2 * P], k_t[rows, a, 0:2 * P],
                              start=True, stop=True).then_inc(scores_ready, 1)

            def turn_probs(pair, par_):
                t = 2 * pair + par_
                pe.wait_ge(softmax_step, 10 * t + 10)
                for r in range(2):
                    for c in range(3):
                        tr = pe.transpose(pt[r][:, c * P:(c + 1) * P], probs[:, r, c, :], ident)
                tr.then_inc(probs_turned, 1)

            def weigh_values(pair, par_, a, first=False):
                t = 2 * pair + par_
                pe.wait_ge(probs_taken, t + 1)
                if not first:
                    pe.wait_ge(out_read, t)
                for r in range(2):
                    rows, head = slice(HD * r, HD * r + HD), slice((2 * a + r) * HD, (2 * a + r + 1) * HD)
                    pr = [probs_t[:, (3 * r + c) * P:(3 * r + c + 1) * P] for c in range(3)]
                    pe.matmul(ot[rows, 0:P], v_p[:, 0, head], pr[0], start=True, stop=True)
                    pe.matmul(ot[rows, P:2 * P], v_p[:, 0, head], pr[1], start=True, stop=False)
                    mm = pe.matmul(ot[rows, P:2 * P], v_p[:, 1, head], pr[2], start=False, stop=True)
                mm.then_inc(out_ready, 1)

            def q_pair(ip, a1, a2):
                scores(ip - 1, 1, a1)
                project_chunk(p, ip, 0, 0, xh, xl)
                weigh_values(ip - 1, 0, a1, first=isinstance(ip, int) and ip == 1)
                project_chunk(p, ip, 0, 1, xh, xl)
                turn_probs(ip - 1, 1)
                scores(ip, 0, a2)
                project_chunk(p, ip, 1, 0, xh, xl)
                weigh_values(ip - 1, 1, a1)
                project_chunk(p, ip, 1, 1, xh, xl)
                turn_probs(ip, 0)

            project_chunk(p, 0, 0, 0, xh, xl)
            turn_v()
            project_chunk(p, 0, 0, 1, xh, xl)
            scores(0, 0, 0, first=True)
            project_group(p, 0, 1, xh, xl)
            turn_probs(0, 0)
            with pe.Fori(1, KD // 4) as ip:
                q_pair(ip, 0, 0)
            q_pair(KD // 4, 0, 1)
            with pe.Fori(KD // 4 + 1, KD // 2) as ip:
                q_pair(ip, 1, 1)
            last = KD // 2 - 1
            scores(last, 1, 1)
            weigh_values(last, 0, 1)
            turn_probs(last, 1)
            weigh_values(last, 1, 1)

            pe.wait_ge(cache_loaded, 32)
            for rd in range(NB // 2):
                if rd == 0:
                    pe.wait_ge(bank_read[0], bank_count(p, last))
                    pe.wait_ge(bank_read[1], bank_count(p, last))
                    pe.wait_ge(scores_read, 2 * KD)
                else:
                    pe.wait_ge(s_scores_read, 4 * rd)
                for x in range(2):
                    n = 2 * rd + x
                    new = slice(SEQ + n * NQ, SEQ + (n + 1) * NQ)
                    for a in range(2):
                        for half in range(2):
                            rows = slice(HD * half, HD * half + HD)
                            q = q_s[rows, a, n, :, :].rearrange("p g q -> p (g q)")
                            pe.matmul(sc[x][rows, a * SKEYS:a * SKEYS + WINDOW], q, kc_t[rows, a, n, :],
                                      start=True, stop=True)
                            mm = pe.matmul(sc[x][rows, a * SKEYS + WINDOW:(a + 1) * SKEYS], q, k_t[rows, a, new],
                                           start=True, stop=True)
                    mm.then_inc(s_scores_ready, 1)
                pe.wait_ge(s_step, 9 * rd + 9)
                if rd == 0:
                    pe.wait_ge(probs_taken, KD)
                for u in range(4):
                    pe.transpose(pt[0][:, u * P:(u + 1) * P], probs_s[:, u, 0:WINDOW], ident)
                    tr = pe.transpose(pt[1][0:NQ, u * P:(u + 1) * P], probs_s[:, u, WINDOW:SKEYS], ident)
                tr.then_inc(s_turned, 1)
                pe.wait_ge(s_taken, rd + 1)
                if rd == 0:
                    pe.wait_ge(out_read, KD)
                else:
                    pe.wait_ge(s_out_read, 2 * rd)
                for u in range(4):
                    n, a = 2 * rd + u // 2, u % 2
                    for half in range(2):
                        rows = slice(HD * half, HD * half + HD)
                        head = slice((2 * a + half) * HD, (2 * a + half + 1) * HD)
                        cols = slice(u * P + HD * half, u * P + HD * half + HD)
                        pe.matmul(ot[rows, u * HD:(u + 1) * HD], v_c[:, n, head], probs_t[:, cols],
                                  start=True, stop=False)
                        mm = pe.matmul(ot[rows, u * HD:(u + 1) * HD], v_n[0:NQ, n, head], probs_tn[0:NQ, cols],
                                       start=False, stop=True)
                mm.then_inc(s_out_ready, 1)

            project(ph["w_o"], xh, xl, (rhs_ready, RHS_ATTN))
            norm_mean(3)
            norm_var(3)
            ffn(1, RHS_MIX1)
            norm_mean(4)
            norm_var(4)

        @block.scalar
        def _(act):
            for q in range(4):
                act.dma_start(xr[:, 4 * q:4 * q + 4, :], io["x"][:, 4 * q:4 * q + 4, :]).then_inc(x_loaded[q], 16)

            def split_hi(p, ip, par_, wait=True):
                for j in range(2):
                    slot, n = 2 * par_ + j, p.kt * P
                    act.wait_ge(raw_loaded[slot], 16 * bank_count(p, ip))
                    if wait:
                        act.wait_ge(multiplied, chunk(p, ip, par_, j) - 3)
                    act.copy(w_hi[:, slot, 0:n], w_raw[:, slot, 0:n]).then_inc(hi_ready, 1)

            def split_next(p, ip, par_, end):
                if not end:
                    split_hi(p, ip + 1, par_)
                elif p.name in after:
                    split_hi(after[p.name], 0, par_)

            def pairs(p, body, first=0):
                n = p.groups // 2
                with act.Fori(first, n - 1) as ip:
                    body(ip, False)
                body(n - 1, True)

            def norm_square(n, src):
                def one(k, par_, wait):
                    act.wait_ge(centered, KD * n + k + 1)
                    if wait:
                        act.wait_ge(var_added, KD * n + k - 1)
                    act.activation(work[:, par_, :], src[:, k, :], ACT.Square).then_inc(squared, 1)
                one(0, 0, False)
                one(1, 1, False)
                with act.Fori(1, KD // 2) as kk:
                    one(2 * kk, 0, True)
                    one(2 * kk + 1, 1, True)

            def norm_apply(n, src, fn, g, b, l, rhs):
                act.wait_ge(var_added, KD * (n + 1))
                act.activation(rstd[:, :], ot[:, 0:T], ACT.Sqrt, bias=const("eps")).then_inc(std_ready, 1)
                with act.Fori(0, KD) as k:
                    act.wait_ge(scaled, KD * n + k + 1)
                    gk, bk = par(g)[:, k + KD * l, :], par(b)[:, k + KD * l, :]
                    if rhs is None:
                        act.activation(work_out(k), src[:, k, :], fn, bias=bk, scale=gk).then_inc(y_ready, 1)
                    else:
                        act.activation(xh[:, k, :], src[:, k, :], fn, bias=bk, scale=gk)
                        act.activation(src[:, k, :], src[:, k, :], fn, bias=bk, scale=gk).then_inc(rhs_hi_ready, 1)

            def work_out(k):
                return xr[:, k, :]

            split_hi(ph["w_in"], 0, 0, wait=False)
            for q in range(4):
                act.wait_ge(x_loaded[q], 16)
                with act.Fori(4 * q, 4 * q + 4) as k:
                    act.copy(xh[:, k, :], xr[:, k, :]).then_inc(rhs_hi_ready, 1)
            split_hi(ph["w_in"], 0, 1, wait=False)
            act.wait_ge(tables_loaded, 32)

            p = ph["w_in"]
            act.wait_ge(zero_ready, 1)

            def glu(i, end, first=False):
                split_next(p, i, 0, end)
                act.wait_ge(multiplied, group_done(p, i, 1))
                act.activation(work[:, 0, :], acc[1][:, 0:T], ACT.Sigmoid, bias=par("b_in")[:, i + KD, :]
                               ).then_inc(bank_read[1], 1)
                act.activation(xr[:, i, :], xr[:, i, :], ACT.Identity, bias=par("b_out")[:, i, :], scale=ALPHA)
                split_next(p, i, 1, end)
                act.wait_ge(bank_read[0], bank_count(p, i))
                if not first:
                    act.wait_ge(conv_step, 32 * i)
                    act.wait_ge(state_saved, 16 * i)
                windows = bass.AP(u_pad[:, :].tensor, 0, [u_pad[:, :].ap[0], [SEG, PSEG], [1, SEGW]])
                act.copy(u_seg[:, 0:PSEG, :], windows)
                act.copy(u_seg[:, PSEG:NSEG, HIST:SEGW],
                         u_pad[:, HIST + SEQ:HIST + T].rearrange("p (n q) -> p n q", q=NQ)).then_inc(useg_built, 1)

            act.wait_ge(rhs_ready, KD)
            glu(0, False, first=True)
            pairs(p, glu, first=1)
            norm_square(0, conv_y)
            norm_apply(0, conv_y, ACT.Silu, "norm_g", "norm_b", 0, RHS_CONV)

            def weights_only(p):
                def body(ip, end):
                    for par_ in range(2):
                        split_next(p, ip, par_, end)
                pairs(p, body)

            weights_only(ph["w_out"])
            norm_square(1, xr)
            norm_apply(1, xr, ACT.Identity, "mix_g", "mix_b", 0, RHS_MIX0)

            def ffn(l):
                act.wait_ge(ffn_in_loaded, 16 * (l + 1))
                if l:
                    act.wait_ge(ffn_out_saved, 16 * l)
                    act.wait_ge(kv_saved, 64)
                else:
                    act.wait_ge(state_saved, 16 * KD)
                for h in range(2):
                    p = ph[f"up{l}{h}"]

                    def body(i, end):
                        f, tile = i + HALF * h, i + KF * l + HALF * h
                        taps = par("f_w_dw")[:, tile, :]
                        act.wait_ge(multiplied, group_done(p, i, 0))
                        gate = acc[0][:, 0:T].rearrange("p (s q) -> p s q", q=SEG)
                        act.activation(work[:, 0, :], acc[0][:, 0:T], ACT.Identity, bias=par("f_b_dw")[:, tile, :],
                                       scale=taps[:, 2:3])
                        act.copy(gate_s[:, :, FW - 1:FW - 1 + NQ], gate[:, PSEG:NSEG, :])
                        act.copy(gate_s[:, :, 0:FW - 1], ffn_in[:, f, :, :])
                        act.copy(ffn_out[:, f, :, :], gate[:, PSEG - 1:NSEG, SEG - (FW - 1):SEG]
                                 ).then_inc(gate_taken, 1)
                        split_next(p, i, 0, end)
                        act.wait_ge(bank_read[0], bank_count(p, i))
                        act.activation(work[:, 0, :], work[:, 0, :], ACT.Gelu).then_inc(gelu_done, 1)
                        act.wait_ge(bank_read[1], bank_count(p, i))
                        act.copy(hh[:, i, :], work[:, 1, :]).then_inc(h_hi_ready, 1)
                        split_next(p, i, 1, end)

                    pairs(p, body)
                    weights_only(ph[f"down{l}{h}"])

            ffn(0)
            norm_square(2, xr)
            norm_apply(2, xr, ACT.Identity, "ffn_g", "ffn_b", 0, RHS_FFN0)
            weights_only(ph["w_kv"])

            p = ph["w_q"]

            def take_probs(pair, par_):
                t = 2 * pair + par_
                act.wait_ge(probs_turned, t + 1)
                act.copy(probs_t[:, 0:3 * P], pt[0][:, 0:3 * P])
                act.copy(probs_t[:, 3 * P:6 * P], pt[1][:, 0:3 * P]).then_inc(probs_taken, 1)

            def exponentials(pair, par_, a):
                t = 2 * pair + par_
                act.wait_ge(softmax_step, 10 * t + 4)
                for r in range(2):
                    act.activation(probs[:, r, 0, :], probs[:, r, 0, :], ACT.Exp, bias=negmax[:, 2 * r:2 * r + 1],
                                   accum_out=rowsum[:, 2 * r:2 * r + 1])
                    act.activation(probs[:, r, 1:3, :], probs[:, r, 1:3, :], ACT.Exp,
                                   bias=negmax[:, 2 * r + 1:2 * r + 2], accum_out=rowsum[:, 2 * r + 1:2 * r + 2])
                    ex = act.activation(sinkexp[:, 2 * r:2 * r + 2], negmax[:, 2 * r:2 * r + 2], ACT.Exp,
                                        bias=par("sinks")[:, 8 * a + 8 * r + t, :])
                ex.then_inc(exp_done, 1)

            def q_pair(ip, a1, a2, end=False):
                take_probs(ip - 1, 0)
                split_hi(p, ip, 1)
                exponentials(ip - 1, 1, a1)
                take_probs(ip - 1, 1)
                if not end:
                    split_hi(p, ip + 1, 0)
                else:
                    split_hi(after[p.name], 0, 0)
                exponentials(ip, 0, a2)

            act.wait_ge(v_transposed, 1)
            act.copy(v_p[:, :, :], pt[0][:, :].rearrange("p (b c) -> p b c", b=2))
            for n2, src in enumerate([sc[0], sc[1], pt[1], ot]):
                cp = act.copy(v_n[0:NQ, 2 * n2:2 * n2 + 2, :], src[0:NQ, :].rearrange("p (b c) -> p b c", b=2))
            cp.then_inc(v_taken, 1)
            split_hi(p, 1, 0)
            exponentials(0, 0, 0)
            with act.Fori(1, KD // 4) as ip:
                q_pair(ip, 0, 0)
            q_pair(KD // 4, 0, 1)
            with act.Fori(KD // 4 + 1, KD // 2 - 1) as ip:
                q_pair(ip, 1, 1)
            last = KD // 2 - 1
            q_pair(last, 1, 1, end=True)
            take_probs(last, 0)
            split_hi(after[p.name], 0, 1)
            exponentials(last, 1, 1)
            take_probs(last, 1)

            act.wait_ge(kv_saved, 64)
            for rd in range(NB // 2):
                act.wait_ge(s_step, 9 * rd + 3)
                for u in range(4):
                    act.activation(probs_s[:, u, :], probs_s[:, u, :], ACT.Exp, bias=negmax[:, u:u + 1],
                                   accum_out=rowsum[:, u:u + 1])
                for a in range(2):
                    ex = act.activation(sinkexp[:, a:a + 3:2], negmax[:, a:a + 3:2], ACT.Exp,
                                        bias=par("sinks_s")[:, a, :])
                ex.then_inc(s_exp_done, 1)
                act.wait_ge(s_turned, rd + 1)
                if rd == 0:
                    act.wait_ge(out_ready, KD)
                act.copy(probs_t[:, 0:4 * P], pt[0][:, :])
                act.copy(probs_tn[0:NQ, 0:4 * P], pt[1][0:NQ, :]).then_inc(s_taken, 1)

            act.wait_ge(s_out_read, NB)
            with act.Fori(0, KD) as k:
                act.copy(xh[:, k, :], qo[:, k, :]).then_inc(rhs_hi_ready, 1)
            weights_only(ph["w_o"])
            norm_square(3, xr)
            norm_apply(3, xr, ACT.Identity, "mix_g", "mix_b", 1, RHS_MIX1)
            ffn(1)
            norm_square(4, xr)
            norm_apply(4, xr, ACT.Identity, "ffn_g", "ffn_b", 1, None)

        @block.vector
        def _(dve):
            def split_lo(p, ip, par_):
                for j in range(2):
                    slot, n = 2 * par_ + j, p.kt * P
                    dve.wait_ge(hi_ready, chunk(p, ip, par_, j) + 1)
                    dve.tensor_tensor(w_lo[:, slot, 0:n], w_raw[:, slot, 0:n], w_hi[:, slot, 0:n],
                                      ALU.subtract).then_inc(lo_ready, 1)

            def split_next(p, ip, par_, end):
                if not end:
                    split_lo(p, ip + 1, par_)
                elif p.name in after:
                    split_lo(after[p.name], 0, par_)

            def pairs(p, body, first=0):
                n = p.groups // 2
                with dve.Fori(first, n - 1) as ip:
                    body(ip, False)
                body(n - 1, True)

            def rhs_lo(base, k, src):
                dve.wait_ge(rhs_hi_ready, base + k + 1)
                dve.tensor_tensor(xl[:, k, :], src[:, k, :], xh[:, k, :], ALU.subtract).then_inc(rhs_ready, 1)

            def norm_center(n, src):
                dve.wait_ge(mean_ready, n + 1)
                with dve.Fori(0, KD) as k:
                    dve.tensor_tensor(src[:, k, :], src[:, k, :], st[:, 0:T], ALU.subtract).then_inc(centered, 1)

            def norm_scale(n, src, rhs):
                dve.wait_ge(std_ready, n + 1)
                dve.reciprocal(rstd[:, :], rstd[:, :]).then_inc(rstd_ready, 1)
                dve.wait_ge(rstd_ready, n + 1)

                def scale(k):
                    dve.tensor_tensor(src[:, k, :], src[:, k, :], rstd[:, :], ALU.mult).then_inc(scaled, 1)

                if rhs is None:
                    with dve.Fori(0, KD) as k:
                        scale(k)
                    return
                scale(0)
                scale(1)
                with dve.Fori(0, KD - 2) as k:
                    scale(k + 2)
                    rhs_lo(rhs, k, src)
                rhs_lo(rhs, KD - 2, src)
                rhs_lo(rhs, KD - 1, src)

            dve.memset(u_pad[:, 0:HIST], 0.0).then_inc(zero_ready, 1)
            split_lo(ph["w_in"], 0, 0)
            with dve.Fori(0, KD) as k:
                rhs_lo(RHS_X, k, xr)
            split_lo(ph["w_in"], 0, 1)
            dve.wait_ge(tables_loaded, 32)

            p = ph["w_in"]

            def conv(i, end):
                split_next(p, i, 0, end)
                dve.wait_ge(bank_read[1], bank_count(p, i))
                dve.scalar_tensor_tensor(u_pad[:, HIST:HIST + T], acc[0][:, 0:T], par("b_in")[:, i, :], work[:, 0, :],
                                         ALU.add, ALU.mult).then_inc(bank_read[0], 1)
                split_next(p, i, 1, end)
                dve.wait_ge(useg_built, i + 1)
                dve.wait_ge(state_loaded, 16 * i + 16)
                even = conv_y[:, i, :].rearrange("p (s q) -> p s q", q=SEG)
                odd = taps_odd[:, :].rearrange("p (s q) -> p s q", q=SEG)
                w = par("w_dw")[:, i, :]
                dve.tensor_scalar(even, u_seg[:, :, 0:SEG], w[:, 0:1], par("b_dw")[:, i, :], ALU.mult, ALU.add
                                  ).then_inc(conv_step, 1)
                dve.tensor_scalar(odd, u_seg[:, :, 1:1 + SEG], w[:, 1:2], None, ALU.mult).then_inc(conv_step, 1)
                for tap in range(2, CW):
                    dst = odd if tap % 2 else even
                    dve.wait_ge(conv_step, 32 * i + tap - 1)
                    dve.scalar_tensor_tensor(dst, u_seg[:, :, tap:tap + SEG], w[:, tap:tap + 1], dst,
                                             ALU.mult, ALU.add).then_inc(conv_step, 1)
                dve.wait_ge(conv_step, 32 * i + CW)
                dve.tensor_tensor(even, even, odd, ALU.add).then_inc(conv_step, 1)

            pairs(p, conv)
            norm_center(0, conv_y)
            norm_scale(0, conv_y, RHS_CONV)

            def residual(p, scale, n_norm):
                def body(ip, end, first=False):
                    for par_ in range(2):
                        k = 2 * ip + par_
                        dve.wait_ge(multiplied, group_done(p, ip, par_))
                        dve.scalar_tensor_tensor(xr[:, k, :], xr[:, k, :], scale, acc[par_][:, 0:T],
                                                 ALU.mult, ALU.add).then_inc(bank_read[par_], 1)
                        final = end and par_ == 1
                        if not final:
                            split_next(p, ip, par_, end)
                        if n_norm and not (first and par_ == 0):
                            dve.wait_ge(bank_read[par_], bank_count(p, ip))
                            if first:
                                dve.tensor_tensor(acc_sum[:, :], xr[:, 0, :], xr[:, 1, :], ALU.add
                                                  ).then_inc(sum_added, 1)
                            else:
                                dve.wait_ge(sum_added, (KD - 1) * (n_norm - 1) + k - 1)
                                dve.tensor_tensor(acc_sum[:, :], acc_sum[:, :], xr[:, k, :], ALU.add
                                                  ).then_inc(sum_added, 1)
                body(0, False, first=True)
                pairs(p, body, first=1)

            def finish_norm(p, n, rhs):
                norm_center(n, xr)
                split_next(p, 0, 1, True)
                norm_scale(n, xr, rhs)

            residual(ph["w_out"], 1.0, 1)
            finish_norm(ph["w_out"], 1, RHS_MIX0)

            def ffn(l, n_norm, rhs):
                if l:
                    dve.wait_ge(kv_saved, 64)
                else:
                    dve.wait_ge(state_saved, 16 * KD)
                for h in range(2):
                    p = ph[f"up{l}{h}"]

                    def body(i, end):
                        tile = i + KF * l + HALF * h
                        taps = par("f_w_dw")[:, tile, :]
                        gy = work[:, 0, :]
                        gy_s = work[:, 0, SEQ:T].rearrange("p (n q) -> p n q", q=NQ)
                        dve.wait_ge(gate_taken, tile + 1)
                        dve.scalar_tensor_tensor(gy[:, 1:SEQ], acc[0][:, 0:SEQ - 1], taps[:, 1:2], gy[:, 1:SEQ],
                                                 ALU.mult, ALU.add).then_inc(taps_done, 1)
                        dve.scalar_tensor_tensor(gy_s, gate_s[:, :, 1:1 + NQ], taps[:, 1:2], gy_s,
                                                 ALU.mult, ALU.add).then_inc(taps_done, 1)
                        dve.wait_ge(taps_done, 3 * tile + 1)
                        dve.scalar_tensor_tensor(gy[:, 2:SEQ], acc[0][:, 0:SEQ - 2], taps[:, 0:1], gy[:, 2:SEQ],
                                                 ALU.mult, ALU.add).then_inc(taps_done, 1)
                        dve.wait_ge(taps_done, 3 * tile + 2)
                        dve.scalar_tensor_tensor(gy_s, gate_s[:, :, 0:NQ], taps[:, 0:1], gy_s,
                                                 ALU.mult, ALU.add).then_inc(bank_read[0], 1)
                        split_next(p, i, 0, end)
                        dve.wait_ge(multiplied, group_done(p, i, 1))
                        dve.wait_ge(gelu_done, tile + 1)
                        dve.tensor_tensor(work[:, 1, :], gy, acc[1][:, 0:T], ALU.mult).then_inc(bank_read[1], 1)
                        split_next(p, i, 1, end)
                        dve.wait_ge(h_hi_ready, tile + 1)
                        dve.tensor_tensor(hl[:, i, :], work[:, 1, :], hh[:, i, :], ALU.subtract).then_inc(h_ready, 1)

                    pairs(p, body)
                    down = ph[f"down{l}{h}"]
                    residual_half(down, ALPHA if h == 0 else 1.0, n_norm if h else 0)
                finish_norm(ph[f"down{l}1"], n_norm, rhs)

            def residual_half(p, scale, n_norm):
                residual(p, scale, n_norm)
                if not n_norm:
                    split_next(p, 0, 1, True)

            ffn(0, 2, RHS_FFN0)

            p = ph["w_kv"]
            for ip, dst in enumerate([k_t, v_t]):
                for par_ in range(2):
                    dve.wait_ge(multiplied, group_done(p, ip, par_))
                    dve.tensor_copy(dst[:, par_, :], acc[par_][:, 0:T]).then_inc(bank_read[par_], 1)
                    split_next(p, ip, par_, ip == 1)

            p = ph["w_q"]

            def softmax_max(pair, par_, a):
                t = 2 * pair + par_
                if not (isinstance(t, int) and t == 0):
                    dve.wait_ge(probs_turned, t)
                dist = const("dist").rearrange("p a b -> p (a b)")
                for r in range(2):
                    dve.wait_ge(scores_ready, 2 * t + r + 1)
                    dve.scalar_tensor_tensor(probs[:, r, :, :].rearrange("p a b -> p (a b)"), dist,
                                             const("negslope")[:, 8 * a + 8 * r + t, :], sc[r][:, 0:3 * P],
                                             ALU.mult, ALU.add).then_inc(scores_read, 1)
                dve.wait_ge(scores_read, 2 * t + 2)
                dve.tensor_reduce(rowmax, probs[:, :, :, :].rearrange("p a b c -> p (a b) c"), AXX, ALU.max
                                  ).then_inc(softmax_step, 1)
                dve.wait_ge(softmax_step, 10 * t + 1)
                rm = rowmax.rearrange("p (r c) -> p r c", c=3)
                dve.tensor_tensor(rm[:, :, 1:2], rm[:, :, 1:2], rm[:, :, 2:3], ALU.max).then_inc(softmax_step, 1)
                dve.wait_ge(softmax_step, 10 * t + 2)
                for r in range(2):
                    dve.tensor_scalar(negmax[:, 2 * r:2 * r + 2], rm[:, r, 0:2], par("sinks")[:, 8 * a + 8 * r + t, :],
                                      -1.0, ALU.max, ALU.mult).then_inc(softmax_step, 1)

            def softmax_divide(pair, par_):
                t = 2 * pair + par_
                dve.wait_ge(exp_done, t + 1)
                dve.tensor_tensor(denom, rowsum, sinkexp, ALU.add).then_inc(softmax_step, 1)
                dve.wait_ge(softmax_step, 10 * t + 5)
                dve.reciprocal(rdenom, denom).then_inc(softmax_step, 1)
                dve.wait_ge(softmax_step, 10 * t + 6)
                for r in range(2):
                    dve.tensor_scalar(probs[:, r, 0, :], probs[:, r, 0, :], rdenom[:, 2 * r:2 * r + 1], None,
                                      ALU.mult).then_inc(softmax_step, 1)
                    dve.tensor_scalar(probs[:, r, 1:3, :], probs[:, r, 1:3, :], rdenom[:, 2 * r + 1:2 * r + 2], None,
                                      ALU.mult).then_inc(softmax_step, 1)

            def take_out(pair, par_):
                t = 2 * pair + par_
                dve.wait_ge(out_ready, t + 1)
                dve.tensor_copy(qo[:, t, 0:SEQ], ot[:, 0:SEQ]).then_inc(out_read, 1)

            def take_q(ip, par_, a):
                dve.wait_ge(multiplied, group_done(p, ip, par_))
                dve.tensor_scalar(q_st[:, par_, :], acc[par_][:, 0:SEQ], QSCALE, None, ALU.mult)
                dve.tensor_scalar(q_s[:, a, :, 2 * ip + par_ - 8 * a, :],
                                  acc[par_][:, SEQ:T].rearrange("p (n q) -> p n q", q=NQ), QSCALE, None, ALU.mult
                                  ).then_inc(bank_read[par_], 1)

            def q_pair(ip, a1, a2, end=False):
                softmax_max(ip - 1, 1, a1)
                split_lo(p, ip, 1)
                softmax_divide(ip - 1, 1)
                take_out(ip - 1, 0)
                take_q(ip, 0, a2)
                softmax_max(ip, 0, a2)
                if not end:
                    split_lo(p, ip + 1, 0)
                else:
                    split_lo(after[p.name], 0, 0)
                softmax_divide(ip, 0)
                take_out(ip - 1, 1)
                take_q(ip, 1, a2)

            take_q(0, 0, 0)
            softmax_max(0, 0, 0)
            split_lo(p, 1, 0)
            softmax_divide(0, 0)
            take_q(0, 1, 0)
            with dve.Fori(1, KD // 4) as ip:
                q_pair(ip, 0, 0)
            q_pair(KD // 4, 0, 1)
            with dve.Fori(KD // 4 + 1, KD // 2 - 1) as ip:
                q_pair(ip, 1, 1)
            last = KD // 2 - 1
            q_pair(last, 1, 1, end=True)
            softmax_max(last, 1, 1)
            split_lo(after[p.name], 0, 1)
            softmax_divide(last, 1)
            take_out(last, 0)
            take_out(last, 1)

            for rd in range(NB // 2):
                if rd == 0:
                    dve.wait_ge(probs_turned, KD)
                else:
                    dve.wait_ge(s_turned, rd)
                for u in range(4):
                    dve.wait_ge(s_scores_ready, 2 * rd + u // 2 + 1)
                    a = u % 2
                    dve.scalar_tensor_tensor(probs_s[:, u, :], const("dist_s"), const("negslope_s")[:, a, :],
                                             sc[u // 2][:, a * SKEYS:(a + 1) * SKEYS], ALU.mult, ALU.add
                                             ).then_inc(s_scores_read, 1)
                dve.wait_ge(s_scores_read, 4 * rd + 4)
                dve.tensor_reduce(rowmax[:, 0:4], probs_s, AXX, ALU.max).then_inc(s_step, 1)
                dve.wait_ge(s_step, 9 * rd + 1)
                for a in range(2):
                    dve.tensor_scalar(negmax[:, a:a + 3:2], rowmax[:, a:a + 3:2], par("sinks_s")[:, a, :], -1.0,
                                      ALU.max, ALU.mult).then_inc(s_step, 1)
                dve.wait_ge(s_exp_done, rd + 1)
                dve.tensor_tensor(denom, rowsum, sinkexp, ALU.add).then_inc(s_step, 1)
                dve.wait_ge(s_step, 9 * rd + 4)
                dve.reciprocal(rdenom, denom).then_inc(s_step, 1)
                dve.wait_ge(s_step, 9 * rd + 5)
                for u in range(4):
                    dve.tensor_scalar(probs_s[:, u, :], probs_s[:, u, :], rdenom[:, u:u + 1], None, ALU.mult
                                      ).then_inc(s_step, 1)
                dve.wait_ge(s_out_ready, rd + 1)
                for x in range(2):
                    n = 2 * rd + x
                    dve.tensor_copy(qo[:, :, SEQ + n * NQ:SEQ + (n + 1) * NQ],
                                    ot[:, x * P:(x + 1) * P].rearrange("p (t q) -> p t q", q=NQ)
                                    ).then_inc(s_out_read, 1)

            with dve.Fori(0, KD) as k:
                rhs_lo(RHS_ATTN, k, qo)
            residual(ph["w_o"], ALPHA, 3)
            finish_norm(ph["w_o"], 3, RHS_MIX1)
            ffn(1, 4, None)



_OUT = {
    "y": (P, KD, T),
    "conv_state_out": (P, KD, NB + 1, HIST),
    "ffn_state_out": (LAYERS, P, KF, NB + 1, FW - 1),
    "k_new": (P, 2, T),
    "v_new": (P, 2, T),
    "kc_out": (NB, WINDOW - NQ, 4 * HD),
    "vc_out": (NB, WINDOW - NQ, 4 * HD),
}


def _stream(w):
    k, n = w.shape
    return w.reshape(k // P, P, n // P, P).transpose(2, 1, 0, 3).reshape(n // P, P, k)


def _feature_tiles(v):
    v = v.reshape(v.shape[:-1] + (v.shape[-1] // P, P))
    return np.moveaxis(np.moveaxis(v, -1, 0), -1, 1)


def _pack(table, values):
    cols = []
    for name, shape in table:
        v = np.asarray(values[name], np.float32)
        cols.append(np.broadcast_to(v, (P,) + v.shape[1:]).reshape(P, -1))
    return np.concatenate(cols, axis=1)


def _constants():
    row = np.arange(P, dtype=np.float32)[:, None]
    col = np.arange(P, dtype=np.float32)[None, :]
    own = np.where(row >= col, row - col, MASKED)
    before = np.where(col >= row, WINDOW + row - col, MASKED)
    q = (np.arange(P) % NQ).astype(np.float32)[:, None]
    key = np.arange(SKEYS, dtype=np.float32)[None, :]
    d = WINDOW + q - key
    slopes = np.float32(2.0) ** (np.float32(-8.0) * np.arange(1, NH + 1, dtype=np.float32) / np.float32(NH))
    return {
        "ident": np.eye(P), "ones_mean": np.full((P, P), 1.0 / D), "dist": np.stack([own, before, own], axis=1),
        "dist_s": np.where((d >= 0) & (d <= WINDOW), d, MASKED),
        "eps": np.full((P, 1), EPS), "negslope": -slopes[None, :, None],
        "negslope_s": -np.repeat(slopes.reshape(2, 2 * 8), NQ, axis=1).T[:, :, None],
    }


def kernel(**inputs):
    import concourse.bacc as _bacc
    from concourse.bass_utils import run_bass_kernel_spmd as _run

    a = {k: np.asarray(v) for k, v in inputs.items()}
    tokens = np.concatenate([a["x_prompt"].reshape(SEQ, D), a["x_sample"].reshape(NS, D)])
    wq = a["b_w_q"][0].reshape(D, 2, 2, 8, HD).transpose(0, 1, 3, 2, 4).reshape(D, D)
    wo = a["b_w_o"][0].reshape(2, 2, 8, HD, D).transpose(0, 2, 1, 3, 4).reshape(D, D)

    arrays = {"x": _feature_tiles(tokens.T[None].transpose(0, 2, 1))[:, :, 0]}
    w_in = _stream(a["a_w_in"][0])
    arrays["w_in"] = w_in.reshape(2, KD, P, D).transpose(1, 0, 2, 3).reshape(2 * KD, P, D)
    arrays["w_out"] = _stream(a["a_w_out"][0])
    arrays["w_kv"], arrays["w_q"], arrays["w_o"] = _stream(a["w_kv"]), _stream(wq), _stream(wo)
    for l in range(LAYERS):
        up = _stream(a["f_w_up"][l]).reshape(2, KF, P, D)
        for h in range(2):
            part = slice(h * HALF, (h + 1) * HALF)
            arrays[f"up{l}{h}"] = up[:, part].transpose(1, 0, 2, 3).reshape(2 * HALF, P, D)
            arrays[f"down{l}{h}"] = _stream(a["f_w_down"][l][h * HALF * P:(h + 1) * HALF * P])
    arrays["conv_state"] = _feature_tiles(a["state_conv_a"][0])
    arrays["ffn_state"] = np.stack([_feature_tiles(s) for s in a["state_ffn_conv"]])
    kc = a["cache_k_win"].reshape(NB, WINDOW, 2, P)
    arrays["k_cache_t"] = kc.transpose(3, 2, 0, 1)
    arrays["k_cache"] = a["cache_k_win"].reshape(NB, WINDOW, 4 * HD)
    arrays["v_cache"] = a["cache_v_win"].reshape(NB, WINDOW, 4 * HD)

    def per_layer(v):
        v = np.stack([_feature_tiles(x) for x in v], axis=1)
        return v.reshape(P, -1, 1)

    sinks = a["b_sinks"][0]
    arrays["params"] = _pack(PARAMS, {
        "b_in": _feature_tiles(a["a_b_in"][0])[:, :, None], "w_dw": _feature_tiles(a["a_w_dw"][0]),
        "b_dw": _feature_tiles(a["a_b_dw"][0])[:, :, None], "norm_g": _feature_tiles(a["a_norm_g"][0])[:, :, None],
        "norm_b": _feature_tiles(a["a_norm_b"][0])[:, :, None], "b_out": _feature_tiles(a["a_b_out"][0])[:, :, None],
        "f_w_dw": np.concatenate([_feature_tiles(x) for x in a["f_w_dw"]], axis=1),
        "f_b_dw": per_layer(a["f_b_dw"]), "mix_g": per_layer(a["ln_mix_g"]), "mix_b": per_layer(a["ln_mix_b"]),
        "ffn_g": per_layer(a["ln_ffn_g"]), "ffn_b": per_layer(a["ln_ffn_b"]),
        "sinks": sinks[None, :, None],
        "sinks_s": np.repeat(sinks.reshape(2, 2 * 8), NQ, axis=1).T[:, :, None],
    })
    arrays["consts"] = _pack(CONSTS, _constants())

    nc = _bacc.Bacc("TRN2", target_bir_lowering=False, num_devices=1)
    io, feed = {}, {}
    for name, v in arrays.items():
        v = np.ascontiguousarray(v)
        feed[f"in_{name}"] = v
        io[name] = nc.dram_tensor(f"in_{name}", v.shape, F32, kind="ExternalInput").ap()
    for name, shape in _OUT.items():
        io[name] = nc.dram_tensor(f"out_{name}", shape, F32, kind="ExternalOutput").ap()
    trunk_kernel(nc, io)
    got = _run(nc, [feed], core_ids=[0]).results[0]
    o = {name: got[f"out_{name}"] for name in _OUT}

    def tokens_of(v):
        v = np.moveaxis(np.moveaxis(v, 1, -1), 0, -1)
        return v.reshape(v.shape[:-2] + (-1,))

    y = tokens_of(o["y"])
    conv = tokens_of(o["conv_state_out"])
    ffn = np.stack([tokens_of(v) for v in o["ffn_state_out"]])
    new = [tokens_of(o["k_new"]), tokens_of(o["v_new"])]
    win_p = [v[SEQ - WINDOW:SEQ].reshape(1, WINDOW, 4, HD) for v in new]
    win_s = [np.concatenate([old, v[SEQ:].reshape(NB, NQ, 4 * HD)], axis=1).reshape(NB, WINDOW, 4, HD)
             for old, v in zip([o["kc_out"], o["vc_out"]], new)]
    return (y[:SEQ].reshape(1, SEQ, D), y[SEQ:].reshape(NB, NQ, D), conv[None, 0:1], ffn[:, 0:1],
            win_p[0], win_p[1], conv[None, 1:], ffn[:, 1:], win_s[0], win_s[1])
```

```python
from contextlib import ExitStack, nullcontext
from collections import namedtuple

import numpy as np

import concourse.bass as bass
from concourse import mybir

F32 = mybir.dt.float32
F32R = mybir.dt.float32r
ALU = mybir.AluOpType
ACT = mybir.ActivationFunctionType
AXX = mybir.AxisListType.X

P = 128
D = 2048
KD = D // P
SEQ = 256
NB, NQ = 8, 8
NS = NB * NQ
T = SEQ + NS
DFF = 5632
KF = DFF // P
HALF = KF // 2
LAYERS = 2
CW = 31
HIST = CW - 1
FW = 3
SEG = 8
NSEG = T // SEG
PSEG = SEQ // SEG
SEGW = HIST + SEG
HD = 64
NH = 32
WINDOW = 128
SKEYS = WINDOW + NQ
ALPHA = float((2.0 * LAYERS) ** 0.25)
EPS = 1e-5
QSCALE = float(HD ** -0.5)
BATCHES = [(0, 1), (1, 2), (2, 4), (4, 8), (8, 12), (12, 16)]
NBT = len(BATCHES)
POOL_TAPS = 12
DVE_TAPS = CW - POOL_TAPS
MASKED = 1e35

Phase = namedtuple("Phase", "name base groups kt")


def phases():
    out, base = {}, 0
    order = [("w_in", 2 * KD, 8), ("w_out", KD, 8)]
    for l in range(LAYERS):
        if l == 1:
            order += [("w_kv", 4, 8), ("w_q", KD, 8), ("w_o", KD, 8)]
        for h in range(2):
            order += [(f"up{l}{h}", 2 * HALF, 8), (f"down{l}{h}", KD, HALF // 2)]
    for name, groups, kt in order:
        out[name] = Phase(name, base, groups, kt)
        base += groups
    return out


PARAMS = [("b_in", (2 * KD, 1)), ("w_dw", (KD, CW)), ("b_dw", (KD, 1)), ("norm_g", (KD, 1)), ("norm_b", (KD, 1)),
          ("b_out", (KD, 1)), ("f_w_dw", (LAYERS * KF, FW)), ("f_b_dw", (LAYERS * KF, 1)),
          ("mix_g", (LAYERS * KD, 1)), ("mix_b", (LAYERS * KD, 1)), ("ffn_g", (LAYERS * KD, 1)),
          ("ffn_b", (LAYERS * KD, 1)), ("sinks", (NH, 1)), ("sinks_s", (2, 1))]
CONSTS = [("ident", (P,)), ("ones_mean", (P,)), ("ones_tile", (P,)), ("dist", (3, P)), ("dist_s", (SKEYS,)),
          ("negslope", (NH, 1)), ("negslope_s", (2, 1)), ("eps", (1,))]


def columns(table):
    at, out = 0, {}
    for name, shape in table:
        n = int(np.prod(shape))
        out[name] = (at, n, shape)
        at += n
    return out, at


def trunk_kernel(nc, io):
    ph = phases()
    pcols, n_params = columns(PARAMS)
    ccols, n_consts = columns(CONSTS)

    with ExitStack() as ctx:
        def sb(name, shape, dt=F32):
            return ctx.enter_context(nc.sbuf_tensor(name, shape, dt))

        def sem(name):
            return ctx.enter_context(nc.semaphore(name))

        def bank(name):
            return ctx.enter_context(nc.psum_tensor(name, [P, 512], F32))

        xr = sb("xr", [P, KD, T])
        xh = sb("xh", [P, KD, T], F32R)
        xl = sb("xl", [P, KD, T], F32R)
        CHUNK = HALF // 2 * P
        w_raw = sb("w_raw", [P, 4, CHUNK])
        w_hi = sb("w_hi", [P, 4, CHUNK], F32R)
        w_lo = sb("w_lo", [P, 4, CHUNK], F32R)
        params = sb("params", [P, n_params])
        consts = sb("consts", [P, n_consts])
        work = sb("work", [P, 2, T])
        rows4 = sb("rows4", [P, 4, T])
        acc_sum, acc_sq, shift, rstd = (rows4[:, i, :] for i in range(4))
        probs_t = rows4[:, :, :].rearrange("p a b -> p (a b)")[:, 0:6 * P]
        ffn_in = sb("ffn_in", [P, KF, NB, FW - 1])
        ffn_out = sb("ffn_out", [P, KF, NB + 1, FW - 1])
        gate_s = sb("gate_s", [P, NB, FW - 1 + NQ])
        with nc.sbuf_tensor("conv_y", [P, KD, T], F32) as conv_y, \
                nc.sbuf_tensor("u_pad", [P, HIST + T], F32) as u_pad, \
                nc.sbuf_tensor("u_seg", [P, NSEG, SEGW], F32) as u_seg, \
                nc.sbuf_tensor("hist", [P, KD, NB, HIST], F32) as hist, \
                nc.sbuf_tensor("prods", [P, POOL_TAPS, T], F32) as prods, \
                nc.sbuf_tensor("taps_pool", [P, T], F32) as taps_pool, \
                nc.sbuf_tensor("taps_part", [P, T], F32) as taps_part:
            pass
        with nc.sbuf_tensor("k_t", [P, 2, T], F32) as k_t, \
                nc.sbuf_tensor("kc_t", [P, 2, NB, WINDOW], F32) as kc_t, \
                nc.sbuf_tensor("v_c", [P, NB, 4 * HD], F32) as v_c, \
                nc.sbuf_tensor("v_p", [P, 2, 4 * HD], F32) as v_p, \
                nc.sbuf_tensor("v_n", [P, NB, 4 * HD], F32) as v_n, \
                nc.sbuf_tensor("qo", [P, KD, T], F32) as qo, \
                nc.sbuf_tensor("q_st", [P, 2, SEQ], F32) as q_st, \
                nc.sbuf_tensor("q_s", [P, 2, NB, 8, NQ], F32) as q_s, \
                nc.sbuf_tensor("probs", [P, 2, 3, P], F32) as probs, \
                nc.sbuf_tensor("smx", [P, 6, 6], F32) as smx:
            pass
        hh = sb("hh", [P, HALF, T], F32R)
        hl = sb("hl", [P, HALF, T], F32R)

        acc = [bank("acc0"), bank("acc1")]
        sc = [bank("sc0"), bank("sc1")]
        pt = [bank("pt0"), bank("pt1")]
        ot = bank("ot")
        st = bank("st")

        def par(name):
            a, n, shape = pcols[name]
            return params[:, a:a + n].rearrange("p (i t) -> p i t", t=shape[1])

        def const(name):
            a, n, shape = ccols[name]
            v = consts[:, a:a + n]
            return v.rearrange("p (i t) -> p i t", t=shape[1]) if len(shape) == 2 else v

        ident, ones_mean, ones_tile = const("ident"), const("ones_mean"), const("ones_tile")
        v_t = work[:, :, :]
        probs_s = probs[:, :, :, :].rearrange("p a b c -> p (a b c)")[:, 0:4 * SKEYS].rearrange(
            "p (u k) -> p u k", u=4)
        probs_tn = work[:, :, :].rearrange("p a b -> p (a b)")
        rowmax, negmax = smx[:, 0, :], smx[:, 1, 0:4]
        rowsum, sinkexp = smx[:, 2, 0:4], smx[:, 3, 0:4]
        denom, rdenom = smx[:, 4, 0:4], smx[:, 5, 0:4]

        raw_loaded = [sem(f"raw_loaded{s}") for s in range(4)]
        hi_ready, lo_ready = sem("hi_ready"), sem("lo_ready")
        multiplied = sem("multiplied")
        bank_read = [sem("bank_read0"), sem("bank_read1")]
        x_loaded = [sem(f"x_loaded{b}") for b in range(NBT)]
        tables_loaded = sem("tables_loaded")
        rhs_hi_ready, rhs_ready = sem("rhs_hi_ready"), sem("rhs_ready")
        zero_ready = sem("zero_ready")
        hist_loaded, state_saved, useg_built = sem("hist_loaded"), sem("state_saved"), sem("useg_built")
        prod_ready, parts_joined = sem("prod_ready"), sem("parts_joined")
        dve_taps, pool_taps, conv0_done = sem("dve_taps"), sem("pool_taps"), sem("conv0_done")
        shift_ready, shift_taken, shifted = sem("shift_ready"), sem("shift_taken"), sem("shifted")
        squared, square_added = sem("squared"), sem("square_added")
        sum_added, sq_added = sem("sum_added"), sem("sq_added")
        mean_ready, mean_squared, moments_ready = sem("mean_ready"), sem("mean_squared"), sem("moments_ready")
        var_ready, std_ready, rstd_ready = sem("var_ready"), sem("std_ready"), sem("rstd_ready")
        centered, scaled, applied = sem("centered"), sem("scaled"), sem("applied")
        ffn_in_loaded, ffn_out_saved = sem("ffn_in_loaded"), sem("ffn_out_saved")
        gate_taken, taps_done, gelu_done = sem("gate_taken"), sem("taps_done"), sem("gelu_done")
        h_hi_ready, h_ready = sem("h_hi_ready"), sem("h_ready")
        cache_loaded, kv_saved = sem("cache_loaded"), sem("kv_saved")
        v_transposed, v_taken = sem("v_transposed"), sem("v_taken")
        scores_ready, scores_read, softmax_step = sem("scores_ready"), sem("scores_read"), sem("softmax_step")
        exp_done, probs_turned, probs_taken = sem("exp_done"), sem("probs_turned"), sem("probs_taken")
        out_ready, out_read = sem("out_ready"), sem("out_read")
        s_scores_ready, s_scores_read, s_step = sem("s_scores_ready"), sem("s_scores_read"), sem("s_step")
        s_exp_done, s_turned, s_taken = sem("s_exp_done"), sem("s_turned"), sem("s_taken")
        s_out_ready, s_out_read = sem("s_out_ready"), sem("s_out_read")
        y_saved = sem("y_saved")

        def chunk(p, ip, par_, j):
            return 2 * p.base + 4 * ip + 2 * par_ + j

        def group_done(p, ip, par_):
            return chunk(p, ip, par_, 0) + 2

        def bank_count(p, ip):
            return p.base // 2 + ip + 1

        RHS_X, RHS_CONV, RHS_MIX0, RHS_FFN0, RHS_ATTN, RHS_MIX1 = (NBT * e for e in range(6))

        def batch_of(k):
            return next(b for b, (lo, hi) in enumerate(BATCHES) if lo <= k < hi)
        order = list(ph.values())
        after = {a.name: b for a, b in zip(order, order[1:])}

        block = ctx.enter_context(nc.Block())

        @block.sync
        def _(sp):
            def load(p, ip, par_, wait=True):
                for j in range(2):
                    slot, n = 2 * par_ + j, p.kt * P
                    if wait:
                        sp.wait_ge(lo_ready, chunk(p, ip, par_, j) - 3)
                    sp.dma_start(w_raw[:, slot, 0:n], io[p.name][2 * ip + par_, :, j * n:(j + 1) * n]
                                 ).then_inc(raw_loaded[slot], 16)

            for p in order:
                first = 0
                if p.base == 0:
                    first = 1
                    load(p, 0, 0, wait=False)
                    load(p, 0, 1, wait=False)
                    sp.dma_start(params[:, :], io["params"]).then_inc(tables_loaded, 16)
                    sp.dma_start(consts[:, :], io["consts"]).then_inc(tables_loaded, 16)
                    sp.dma_start(hist[:, :, :, :], io["conv_state"]).then_inc(hist_loaded, 16)
                with sp.Fori(first, p.groups // 2) as ip:
                    load(p, ip, 0)
                    load(p, ip, 1)
            for lo, hi in BATCHES[2:]:
                lo = 0 if lo == 2 else lo
                sp.wait_ge(applied, 4 * KD + hi)
                sp.dma_start(io["y"][:, lo:hi, :], xr[:, lo:hi, :]).then_inc(y_saved, 16)
            sp.wait_ge(y_saved, 16 * (NBT - 2))

        @block.gpsimd
        def _(pool):
            pool.dma_start(ffn_in[:, :, :, :], io["ffn_state"][0]).then_inc(ffn_in_loaded, 16)
            pool.dma_start(io["kc_out"], io["k_cache"][:, NQ:WINDOW, :]).then_inc(kv_saved, 16)
            pool.dma_start(io["vc_out"], io["v_cache"][:, NQ:WINDOW, :]).then_inc(kv_saved, 16)

            def conv_taps(i, first=False):
                if not first:
                    pool.wait_ge(shift_taken, 1)
                    pool.wait_ge(parts_joined, i)
                for n in range(POOL_TAPS):
                    pool.wait_ge(prod_ready, POOL_TAPS * i + n + 1)
                    if n:
                        pool.wait_ge(pool_taps, POOL_TAPS * i + n)
                    pool.tensor_tensor(taps_pool[:, :], prods[:, n, :], taps_pool[:, :] if n else shift, ALU.add
                                       ).then_inc(pool_taps, 1)

            pool.wait_ge(zero_ready, 2)
            conv_taps(0, first=True)
            with pool.Fori(1, KD) as i:
                conv_taps(i)

            pool.wait_ge(h_ready, KF)
            pool.dma_start(io["ffn_state_out"][0], ffn_out[:, :, :, :]).then_inc(ffn_out_saved, 16)
            pool.dma_start(ffn_in[:, :, :, :], io["ffn_state"][1]).then_inc(ffn_in_loaded, 16)
            pool.wait_ge(multiplied, 2 * ph["w_kv"].base)
            pool.dma_start(kc_t[:, :, :, :], io["k_cache_t"]).then_inc(cache_loaded, 16)
            pool.dma_start(v_c[:, :, :], io["v_cache"].rearrange("n k c -> k n c")).then_inc(cache_loaded, 16)
            pool.wait_ge(bank_read[0], bank_count(ph["w_kv"], 1))
            pool.wait_ge(bank_read[1], bank_count(ph["w_kv"], 1))
            pool.dma_start(io["k_new"], k_t[:, :, :]).then_inc(kv_saved, 16)
            pool.dma_start(io["v_new"], v_t).then_inc(kv_saved, 16)
            pool.wait_ge(h_ready, 2 * KF)
            pool.dma_start(io["ffn_state_out"][1], ffn_out[:, :, :, :]).then_inc(ffn_out_saved, 16)
            pool.wait_ge(state_saved, 16 * KD)
            pool.wait_ge(kv_saved, 64)
            pool.wait_ge(ffn_out_saved, 32)

        @block.tensor
        def _(pe):
            def project_chunk(p, ip, par_, j, hi, lo, rhs_wait=None):
                slot = 2 * par_ + j
                if j == 0 and not (p.base == 0 and isinstance(ip, int) and ip == 0):
                    pe.wait_ge(bank_read[par_], bank_count(p, ip) - 1)
                pe.wait_ge(lo_ready, chunk(p, ip, par_, j) + 1)
                for i in range(p.kt):
                    k = j * p.kt + i
                    if rhs_wait is not None:
                        pe.wait_ge(rhs_wait[0], rhs_wait[1] + k + 1)
                    wh, wl = w_hi[:, slot, i * P:(i + 1) * P], w_lo[:, slot, i * P:(i + 1) * P]
                    out = acc[par_][:, 0:T]
                    first, last = k == 0, k == 2 * p.kt - 1
                    pe.matmul(out, wh, hi[:, k, :], start=first, stop=False)
                    pe.matmul(out, wh, lo[:, k, :], start=False, stop=False)
                    mm = pe.matmul(out, wl, hi[:, k, :], start=False, stop=last)
                mm.then_inc(multiplied, 1)

            def project_group(p, ip, par_, hi, lo, rhs_wait=None):
                for j in range(2):
                    project_chunk(p, ip, par_, j, hi, lo, rhs_wait)

            def project_first_pair(p, hi, lo, event):
                for par_ in range(2):
                    if p.base:
                        pe.wait_ge(bank_read[par_], bank_count(p, 0) - 1)
                for k in range(KD):
                    j, i = k // p.kt, k % p.kt
                    if k == BATCHES[batch_of(k)][0]:
                        pe.wait_ge(rhs_ready, event + batch_of(k) + 1)
                    for par_ in range(2):
                        if i == 0:
                            pe.wait_ge(lo_ready, chunk(p, 0, par_, j) + 1)
                        slot = 2 * par_ + j
                        wh, wl = w_hi[:, slot, i * P:(i + 1) * P], w_lo[:, slot, i * P:(i + 1) * P]
                        out = acc[par_][:, 0:T]
                        pe.matmul(out, wh, hi[:, k, :], start=(k == 0), stop=False)
                        pe.matmul(out, wh, lo[:, k, :], start=False, stop=False)
                        mm = pe.matmul(out, wl, hi[:, k, :], start=False, stop=(k == KD - 1))
                        if i == p.kt - 1:
                            n = {(0, 0): 1, (1, 0): 0, (0, 1): 2, (1, 1): 1}[(par_, j)]
                            if n:
                                mm.then_inc(multiplied, n)

            def project_pairs(p, hi, lo):
                with pe.Fori(1, p.groups // 2) as ip:
                    project_group(p, ip, 0, hi, lo)
                    project_group(p, ip, 1, hi, lo)

            def project(p, hi, lo, rhs_wait):
                project_group(p, 0, 0, hi, lo, rhs_wait)
                project_group(p, 0, 1, hi, lo)
                project_pairs(p, hi, lo)

            def find_shift(p, n):
                pe.wait_ge(bank_read[0], bank_count(p, 0))
                pe.matmul(st[:, 0:T], ones_tile, xr[:, 0, :], start=True, stop=True).then_inc(shift_ready, 1)

            def project_residual(p, hi, lo, n, event=None, rhs_wait=None):
                if event is None:
                    project_group(p, 0, 0, hi, lo, rhs_wait)
                    project_group(p, 0, 1, hi, lo)
                else:
                    project_first_pair(p, hi, lo, event)
                find_shift(p, n)
                project_pairs(p, hi, lo)
                pe.wait_ge(sum_added, (KD - 2) * n)
                pe.wait_ge(shift_taken, n + 1)
                pe.matmul(st[:, 0:T], ones_mean, acc_sum, start=True, stop=False)
                pe.wait_ge(shifted, KD * (n + 1))
                pe.matmul(st[:, 0:T], ones_mean, xr[:, KD - 1, :], start=False, stop=True).then_inc(mean_ready, 1)
                pe.wait_ge(sq_added, (KD - 2) * n)
                pe.matmul(ot[:, 0:T], ones_mean, acc_sq, start=True, stop=False)
                pe.wait_ge(squared, KD * (n + 1))
                pe.matmul(ot[:, 0:T], ones_mean, work[:, 1, :], start=False, stop=True).then_inc(moments_ready, 1)

            p = ph["w_in"]

            def add_moments(i):
                first, last = isinstance(i, int) and i == 0, isinstance(i, int) and i == KD - 1
                pe.wait_ge(shifted, i + 1)
                mm = pe.matmul(st[:, 0:T], ones_mean, conv_y[:, i, :], start=first, stop=last)
                if last:
                    mm.then_inc(mean_ready, 1)
                pe.wait_ge(squared, i + 1)
                pe.matmul(ot[:, 0:T], ones_mean, work[:, 1, :], start=first, stop=last).then_inc(
                    moments_ready if last else square_added, 1)

            project_first_pair(p, xh, xl, RHS_X)
            project_group(p, 1, 0, xh, xl)
            project_group(p, 1, 1, xh, xl)
            pe.wait_ge(tables_loaded, 32)
            pe.wait_ge(conv0_done, 1)
            pe.matmul(pt[0][:, 0:T], ones_tile, conv_y[:, 0, :], start=True, stop=True).then_inc(shift_ready, 1)
            project_group(p, 2, 0, xh, xl)
            project_group(p, 2, 1, xh, xl)
            add_moments(0)
            with pe.Fori(3, KD) as ip:
                project_group(p, ip, 0, xh, xl)
                project_group(p, ip, 1, xh, xl)
                add_moments(ip - 2)
            add_moments(KD - 2)
            add_moments(KD - 1)
            project_residual(ph["w_out"], xh, xl, 1, event=RHS_CONV)

            def ffn(l, event):
                for h in range(2):
                    up, down = ph[f"up{l}{h}"], ph[f"down{l}{h}"]
                    if h == 0:
                        project_first_pair(up, xh, xl, event)
                        project_pairs(up, xh, xl)
                        project(down, hh, hl, (h_ready, KF * l))
                    else:
                        project(up, xh, xl, None)
                        project_residual(down, hh, hl, 2 * l + 2, rhs_wait=(h_ready, KF * l + HALF))

            ffn(0, RHS_MIX0)

            p = ph["w_kv"]
            project_first_pair(p, xh, xl, RHS_FFN0)
            project_group(p, 1, 0, xh, xl)
            project_group(p, 1, 1, xh, xl)

            p = ph["w_q"]

            def turn_v():
                pe.wait_ge(bank_read[0], bank_count(ph["w_kv"], 1))
                pe.wait_ge(bank_read[1], bank_count(ph["w_kv"], 1))
                for b in range(2):
                    for a in range(2):
                        pe.transpose(pt[0][:, b * 256 + a * P:b * 256 + (a + 1) * P],
                                     v_t[:, a, b * P:(b + 1) * P], ident)
                for n in range(NB):
                    dst = [sc[0], sc[1], pt[1], ot][n // 2]
                    for a in range(2):
                        tr = pe.transpose(dst[0:NQ, (n % 2) * 256 + a * P:(n % 2) * 256 + (a + 1) * P],
                                          v_t[:, a, SEQ + n * NQ:SEQ + (n + 1) * NQ], ident)
                tr.then_inc(v_transposed, 1)

            def scores(pair, par_, a, first=False):
                t = 2 * pair + par_
                pe.wait_ge(bank_read[par_], bank_count(p, pair))
                if first:
                    pe.wait_ge(v_taken, 1)
                else:
                    pe.wait_ge(scores_read, 2 * t)
                for r in range(2):
                    rows = slice(HD * r, HD * r + HD)
                    pe.matmul(sc[r][:, 0:P], q_st[rows, par_, 0:P], k_t[rows, a, 0:P], start=True, stop=True)
                    pe.matmul(sc[r][:, P:3 * P], q_st[rows, par_, P:2 * P], k_t[rows, a, 0:2 * P],
                              start=True, stop=True).then_inc(scores_ready, 1)

            def turn_probs(pair, par_):
                t = 2 * pair + par_
                pe.wait_ge(softmax_step, 10 * t + 10)
                for r in range(2):
                    for c in range(3):
                        tr = pe.transpose(pt[r][:, c * P:(c + 1) * P], probs[:, r, c, :], ident)
                tr.then_inc(probs_turned, 1)

            def weigh_values(pair, par_, a, first=False):
                t = 2 * pair + par_
                pe.wait_ge(probs_taken, t + 1)
                if not first:
                    pe.wait_ge(out_read, t)
                for r in range(2):
                    rows, head = slice(HD * r, HD * r + HD), slice((2 * a + r) * HD, (2 * a + r + 1) * HD)
                    pr = [probs_t[:, (3 * r + c) * P:(3 * r + c + 1) * P] for c in range(3)]
                    pe.matmul(ot[rows, 0:P], v_p[:, 0, head], pr[0], start=True, stop=True)
                    pe.matmul(ot[rows, P:2 * P], v_p[:, 0, head], pr[1], start=True, stop=False)
                    mm = pe.matmul(ot[rows, P:2 * P], v_p[:, 1, head], pr[2], start=False, stop=True)
                mm.then_inc(out_ready, 1)

            def q_pair(ip, a1, a2):
                scores(ip - 1, 1, a1)
                project_chunk(p, ip, 0, 0, xh, xl)
                weigh_values(ip - 1, 0, a1, first=isinstance(ip, int) and ip == 1)
                project_chunk(p, ip, 0, 1, xh, xl)
                turn_probs(ip - 1, 1)
                scores(ip, 0, a2)
                project_chunk(p, ip, 1, 0, xh, xl)
                weigh_values(ip - 1, 1, a1)
                project_chunk(p, ip, 1, 1, xh, xl)
                turn_probs(ip, 0)

            project_chunk(p, 0, 0, 0, xh, xl)
            turn_v()
            project_chunk(p, 0, 0, 1, xh, xl)
            scores(0, 0, 0, first=True)
            project_group(p, 0, 1, xh, xl)
            turn_probs(0, 0)
            with pe.Fori(1, KD // 4) as ip:
                q_pair(ip, 0, 0)
            q_pair(KD // 4, 0, 1)
            with pe.Fori(KD // 4 + 1, KD // 2) as ip:
                q_pair(ip, 1, 1)
            last = KD // 2 - 1
            scores(last, 1, 1)
            weigh_values(last, 0, 1)
            turn_probs(last, 1)
            weigh_values(last, 1, 1)

            pe.wait_ge(cache_loaded, 32)
            for rd in range(NB // 2):
                if rd == 0:
                    pe.wait_ge(bank_read[0], bank_count(p, last))
                    pe.wait_ge(bank_read[1], bank_count(p, last))
                    pe.wait_ge(scores_read, 2 * KD)
                else:
                    pe.wait_ge(s_scores_read, 4 * rd)
                for x in range(2):
                    n = 2 * rd + x
                    new = slice(SEQ + n * NQ, SEQ + (n + 1) * NQ)
                    for a in range(2):
                        for half in range(2):
                            rows = slice(HD * half, HD * half + HD)
                            q = q_s[rows, a, n, :, :].rearrange("p g q -> p (g q)")
                            pe.matmul(sc[x][rows, a * SKEYS:a * SKEYS + WINDOW], q, kc_t[rows, a, n, :],
                                      start=True, stop=True)
                            mm = pe.matmul(sc[x][rows, a * SKEYS + WINDOW:(a + 1) * SKEYS], q, k_t[rows, a, new],
                                           start=True, stop=True)
                    mm.then_inc(s_scores_ready, 1)
                pe.wait_ge(s_step, 9 * rd + 9)
                if rd == 0:
                    pe.wait_ge(probs_taken, KD)
                for u in range(4):
                    pe.transpose(pt[0][:, u * P:(u + 1) * P], probs_s[:, u, 0:WINDOW], ident)
                    tr = pe.transpose(pt[1][0:NQ, u * P:(u + 1) * P], probs_s[:, u, WINDOW:SKEYS], ident)
                tr.then_inc(s_turned, 1)
                pe.wait_ge(s_taken, rd + 1)
                if rd == 0:
                    pe.wait_ge(out_read, KD)
                else:
                    pe.wait_ge(s_out_read, 2 * rd)
                for u in range(4):
                    n, a = 2 * rd + u // 2, u % 2
                    for half in range(2):
                        rows = slice(HD * half, HD * half + HD)
                        head = slice((2 * a + half) * HD, (2 * a + half + 1) * HD)
                        cols = slice(u * P + HD * half, u * P + HD * half + HD)
                        pe.matmul(ot[rows, u * HD:(u + 1) * HD], v_c[:, n, head], probs_t[:, cols],
                                  start=True, stop=False)
                        mm = pe.matmul(ot[rows, u * HD:(u + 1) * HD], v_n[0:NQ, n, head], probs_tn[0:NQ, cols],
                                       start=False, stop=True)
                mm.then_inc(s_out_ready, 1)

            project_residual(ph["w_o"], xh, xl, 3, event=RHS_ATTN)
            ffn(1, RHS_MIX1)

        @block.scalar
        def _(act):
            for b, (lo, hi) in enumerate(BATCHES):
                act.dma_start(xr[:, lo:hi, :], io["x"][:, lo:hi, :]).then_inc(x_loaded[b], 16)

            def split_hi(p, ip, par_, wait=True, chunks=(0, 1)):
                for j in chunks:
                    slot, n = 2 * par_ + j, p.kt * P
                    act.wait_ge(raw_loaded[slot], 16 * bank_count(p, ip))
                    if wait:
                        act.wait_ge(multiplied, chunk(p, ip, par_, j) - 3)
                    act.copy(w_hi[:, slot, 0:n], w_raw[:, slot, 0:n]).then_inc(hi_ready, 1)

            def split_next(p, ip, par_, end):
                if not end:
                    split_hi(p, ip + 1, par_)
                elif p.name in after:
                    split_hi(after[p.name], 0, par_)

            def pairs(p, body, first=0):
                n = p.groups // 2
                with act.Fori(first, n - 1) as ip:
                    body(ip, False)
                body(n - 1, True)

            def square(n, k, src, dst):
                act.wait_ge(shifted, KD * n + k + 1)
                act.activation(dst, src, ACT.Square).then_inc(squared, 1)

            def norm(n, src, fn, g, b, l, nxt, rhs):
                act.activation(rstd[:, 0:1], const("eps"), ACT.Sqrt)
                act.wait_ge(mean_ready, n + 1)
                act.activation(work[:, 0, :], st[:, 0:T], ACT.Square).then_inc(mean_squared, 1)
                act.wait_ge(var_ready, n + 1)
                act.activation(rstd, rstd, ACT.Sqrt, bias=const("eps")).then_inc(std_ready, 1)
                if nxt:
                    split_hi(nxt, 0, 1, chunks=(1,))
                for bt, (lo, hi) in enumerate(BATCHES):
                    act.wait_ge(scaled, NBT * n + bt + 1)
                    for k in range(lo, hi):
                        act.activation(src[:, k, :], src[:, k, :], fn, bias=par(b)[:, k + KD * l, :],
                                       scale=par(g)[:, k + KD * l, :]).then_inc(applied, 1)
                    if rhs is not None:
                        act.wait_ge(applied, KD * n + hi)
                        act.copy(xh[:, lo:hi, :], src[:, lo:hi, :]).then_inc(rhs_hi_ready, 1)

            split_hi(ph["w_in"], 0, 0, wait=False, chunks=(0,))
            for bt, (lo, hi) in enumerate(BATCHES):
                act.wait_ge(x_loaded[bt], 16)
                act.copy(xh[:, lo:hi, :], xr[:, lo:hi, :]).then_inc(rhs_hi_ready, 1)
                if bt == 0:
                    split_hi(ph["w_in"], 0, 0, wait=False, chunks=(1,))
                if bt == 1:
                    split_hi(ph["w_in"], 0, 1, wait=False, chunks=(0,))
                if bt == 3:
                    split_hi(ph["w_in"], 0, 1, wait=False, chunks=(1,))
            act.wait_ge(tables_loaded, 32)
            act.wait_ge(hist_loaded, 16)

            p = ph["w_in"]
            act.wait_ge(zero_ready, 1)

            def conv_square(i, first=False):
                if not first:
                    act.wait_ge(square_added, i)
                square(0, i, conv_y[:, i, :], work[:, 1, :])

            def glu(i, end, first=False):
                split_next(p, i, 0, end)
                act.wait_ge(multiplied, group_done(p, i, 1))
                act.activation(work[:, 0, :], acc[1][:, 0:T], ACT.Sigmoid, bias=par("b_in")[:, i + KD, :]
                               ).then_inc(bank_read[1], 1)
                split_next(p, i, 1, end)
                act.wait_ge(bank_read[0], bank_count(p, i))
                if not first:
                    act.wait_ge(dve_taps, DVE_TAPS * i)
                    act.wait_ge(prod_ready, POOL_TAPS * i)
                    act.wait_ge(state_saved, 16 * i)
                windows = bass.AP(u_pad[:, :].tensor, 0, [u_pad[:, :].ap[0], [SEG, PSEG], [1, SEGW]])
                act.copy(u_seg[:, 0:PSEG, :], windows)
                act.copy(u_seg[:, PSEG:NSEG, 0:HIST], hist[:, i, :, :])
                act.copy(u_seg[:, PSEG:NSEG, HIST:SEGW],
                         u_pad[:, HIST + SEQ:HIST + T].rearrange("p (n q) -> p n q", q=NQ)).then_inc(useg_built, 1)
                act.wait_ge(useg_built, i + 1)
                act.dma_start(io["conv_state_out"][:, i], u_seg[:, PSEG - 1:NSEG, SEG:SEGW]).then_inc(state_saved, 16)
                if not first:
                    act.wait_ge(pool_taps, POOL_TAPS * i)
                for n in range(POOL_TAPS):
                    tap = DVE_TAPS + n
                    act.activation(prods[:, n, :].rearrange("p (s q) -> p s q", q=SEG), u_seg[:, :, tap:tap + SEG],
                                   ACT.Identity, scale=par("w_dw")[:, i, tap:tap + 1]).then_inc(prod_ready, 1)
                act.activation(xr[:, i, :], xr[:, i, :], ACT.Identity, bias=par("b_out")[:, i, :], scale=ALPHA)

            def glu_and_square(i, end):
                glu(i, end)
                conv_square(i - 1)

            act.wait_ge(rhs_ready, NBT)
            glu(0, False, first=True)
            glu(1, False)
            conv_square(0, first=True)
            pairs(p, glu_and_square, first=2)
            conv_square(KD - 1)
            norm(0, conv_y, ACT.Silu, "norm_g", "norm_b", 0, None, RHS_CONV)

            def weights_only(p):
                def body(ip, end):
                    for par_ in range(2):
                        split_next(p, ip, par_, end)
                pairs(p, body)

            def residual(p, n):
                split_hi(p, 1, 0)
                split_hi(p, 1, 1)
                square(n, 0, xr[:, 0, :], acc_sq)
                square(n, 1, xr[:, 1, :], work[:, 1, :])

                def body(ip, end):
                    split_next(p, ip, 0, end)
                    act.wait_ge(sq_added, (KD - 2) * (n - 1) + 2 * ip - 1)
                    square(n, 2 * ip, xr[:, 2 * ip, :], work[:, 1, :])
                    if not end:
                        split_next(p, ip, 1, end)
                    elif p.name in after:
                        split_hi(after[p.name], 0, 1, chunks=(0,))
                    act.wait_ge(sq_added, (KD - 2) * (n - 1) + 2 * ip)
                    square(n, 2 * ip + 1, xr[:, 2 * ip + 1, :], work[:, 1, :])

                pairs(p, body, first=1)

            residual(ph["w_out"], 1)
            norm(1, xr, ACT.Identity, "mix_g", "mix_b", 0, after["w_out"], RHS_MIX0)

            def ffn(l):
                act.wait_ge(ffn_in_loaded, 16 * (l + 1))
                if l:
                    act.wait_ge(ffn_out_saved, 16 * l)
                    act.wait_ge(kv_saved, 64)
                else:
                    act.wait_ge(state_saved, 16 * KD)
                for h in range(2):
                    p = ph[f"up{l}{h}"]

                    def body(i, end):
                        f, tile = i + HALF * h, i + KF * l + HALF * h
                        taps = par("f_w_dw")[:, tile, :]
                        act.wait_ge(multiplied, group_done(p, i, 0))
                        gate = acc[0][:, 0:T].rearrange("p (s q) -> p s q", q=SEG)
                        act.activation(work[:, 0, :], acc[0][:, 0:T], ACT.Identity, bias=par("f_b_dw")[:, tile, :],
                                       scale=taps[:, 2:3])
                        act.copy(gate_s[:, :, FW - 1:FW - 1 + NQ], gate[:, PSEG:NSEG, :])
                        act.copy(gate_s[:, :, 0:FW - 1], ffn_in[:, f, :, :])
                        act.copy(ffn_out[:, f, :, :], gate[:, PSEG - 1:NSEG, SEG - (FW - 1):SEG]
                                 ).then_inc(gate_taken, 1)
                        split_next(p, i, 0, end)
                        act.wait_ge(bank_read[0], bank_count(p, i))
                        act.activation(work[:, 0, :], work[:, 0, :], ACT.Gelu).then_inc(gelu_done, 1)
                        act.wait_ge(bank_read[1], bank_count(p, i))
                        act.copy(hh[:, i, :], work[:, 1, :]).then_inc(h_hi_ready, 1)
                        split_next(p, i, 1, end)

                    act.activation(rstd[:, 0:1], const("eps"), ACT.Gelu)
                    pairs(p, body)
                    if h == 0:
                        weights_only(ph[f"down{l}{h}"])
                    else:
                        residual(ph[f"down{l}{h}"], 2 * l + 2)

            ffn(0)
            norm(2, xr, ACT.Identity, "ffn_g", "ffn_b", 0, after["down01"], RHS_FFN0)
            weights_only(ph["w_kv"])

            p = ph["w_q"]

            def take_probs(pair, par_):
                t = 2 * pair + par_
                act.wait_ge(probs_turned, t + 1)
                act.copy(probs_t[:, 0:3 * P], pt[0][:, 0:3 * P])
                act.copy(probs_t[:, 3 * P:6 * P], pt[1][:, 0:3 * P]).then_inc(probs_taken, 1)

            def exponentials(pair, par_, a):
                t = 2 * pair + par_
                act.wait_ge(softmax_step, 10 * t + 4)
                for r in range(2):
                    act.activation(probs[:, r, 0, :], probs[:, r, 0, :], ACT.Exp, bias=negmax[:, 2 * r:2 * r + 1],
                                   accum_out=rowsum[:, 2 * r:2 * r + 1])
                    act.activation(probs[:, r, 1:3, :], probs[:, r, 1:3, :], ACT.Exp,
                                   bias=negmax[:, 2 * r + 1:2 * r + 2], accum_out=rowsum[:, 2 * r + 1:2 * r + 2])
                    ex = act.activation(sinkexp[:, 2 * r:2 * r + 2], negmax[:, 2 * r:2 * r + 2], ACT.Exp,
                                        bias=par("sinks")[:, 8 * a + 8 * r + t, :])
                ex.then_inc(exp_done, 1)

            def q_pair(ip, a1, a2, end=False):
                take_probs(ip - 1, 0)
                split_hi(p, ip, 1)
                exponentials(ip - 1, 1, a1)
                take_probs(ip - 1, 1)
                if not end:
                    split_hi(p, ip + 1, 0)
                else:
                    split_hi(after[p.name], 0, 0)
                exponentials(ip, 0, a2)

            act.wait_ge(v_transposed, 1)
            act.copy(v_p[:, :, :], pt[0][:, :].rearrange("p (b c) -> p b c", b=2))
            for n2, src in enumerate([sc[0], sc[1], pt[1], ot]):
                cp = act.copy(v_n[0:NQ, 2 * n2:2 * n2 + 2, :], src[0:NQ, :].rearrange("p (b c) -> p b c", b=2))
            cp.then_inc(v_taken, 1)
            split_hi(p, 1, 0)
            exponentials(0, 0, 0)
            with act.Fori(1, KD // 4) as ip:
                q_pair(ip, 0, 0)
            q_pair(KD // 4, 0, 1)
            with act.Fori(KD // 4 + 1, KD // 2 - 1) as ip:
                q_pair(ip, 1, 1)
            last = KD // 2 - 1
            q_pair(last, 1, 1, end=True)
            take_probs(last, 0)
            split_hi(after[p.name], 0, 1)
            exponentials(last, 1, 1)
            take_probs(last, 1)

            act.wait_ge(kv_saved, 64)
            for rd in range(NB // 2):
                act.wait_ge(s_step, 9 * rd + 3)
                for u in range(4):
                    act.activation(probs_s[:, u, :], probs_s[:, u, :], ACT.Exp, bias=negmax[:, u:u + 1],
                                   accum_out=rowsum[:, u:u + 1])
                for a in range(2):
                    ex = act.activation(sinkexp[:, a:a + 3:2], negmax[:, a:a + 3:2], ACT.Exp,
                                        bias=par("sinks_s")[:, a, :])
                ex.then_inc(s_exp_done, 1)
                act.wait_ge(s_turned, rd + 1)
                if rd == 0:
                    act.wait_ge(out_ready, KD)
                act.copy(probs_t[:, 0:4 * P], pt[0][:, :])
                act.copy(probs_tn[0:NQ, 0:4 * P], pt[1][0:NQ, :]).then_inc(s_taken, 1)

            act.wait_ge(s_out_read, NB)
            for lo, hi in BATCHES:
                act.copy(xh[:, lo:hi, :], qo[:, lo:hi, :]).then_inc(rhs_hi_ready, 1)
            residual(ph["w_o"], 3)
            norm(3, xr, ACT.Identity, "mix_g", "mix_b", 1, after["w_o"], RHS_MIX1)
            ffn(1)
            norm(4, xr, ACT.Identity, "ffn_g", "ffn_b", 1, None, None)

        @block.vector
        def _(dve):
            def split_lo(p, ip, par_, chunks=(0, 1)):
                for j in chunks:
                    slot, n = 2 * par_ + j, p.kt * P
                    dve.wait_ge(hi_ready, chunk(p, ip, par_, j) + 1)
                    dve.tensor_tensor(w_lo[:, slot, 0:n], w_raw[:, slot, 0:n], w_hi[:, slot, 0:n],
                                      ALU.subtract).then_inc(lo_ready, 1)

            def split_next(p, ip, par_, end):
                if not end:
                    split_lo(p, ip + 1, par_)
                elif p.name in after:
                    split_lo(after[p.name], 0, par_)

            def pairs(p, body, first=0):
                n = p.groups // 2
                with dve.Fori(first, n - 1) as ip:
                    body(ip, False)
                body(n - 1, True)

            def rhs_lo(base, bt, src):
                lo, hi = BATCHES[bt]
                dve.wait_ge(rhs_hi_ready, base + bt + 1)
                dve.tensor_tensor(xl[:, lo:hi, :], src[:, lo:hi, :], xh[:, lo:hi, :], ALU.subtract
                                  ).then_inc(rhs_ready, 1)

            def over_tiles(row, n):
                return bass.AP(row.tensor, row.offset, [row.ap[0], [0, n], [1, T]])

            def norm(n, src, nxt, rhs):
                def center(bt):
                    lo, hi = BATCHES[bt]
                    dve.tensor_tensor(src[:, lo:hi, :], src[:, lo:hi, :], over_tiles(st[:, 0:T], hi - lo),
                                      ALU.subtract).then_inc(centered, 1)

                dve.wait_ge(mean_squared, n + 1)
                for bt in range(3):
                    center(bt)
                dve.wait_ge(moments_ready, n + 1)
                dve.tensor_tensor(rstd, ot[:, 0:T], work[:, 0, :], ALU.subtract).then_inc(var_ready, 1)
                center(3)
                dve.wait_ge(std_ready, n + 1)
                dve.reciprocal(rstd, rstd).then_inc(rstd_ready, 1)
                dve.wait_ge(rstd_ready, n + 1)
                for bt, (lo, hi) in enumerate(BATCHES):
                    dve.wait_ge(centered, NBT * n + bt + 1)
                    dve.tensor_tensor(src[:, lo:hi, :], src[:, lo:hi, :], over_tiles(rstd, hi - lo),
                                      ALU.mult).then_inc(scaled, 1)
                    if 2 <= bt and bt + 2 < NBT:
                        center(bt + 2)
                    if rhs is not None and bt >= 2:
                        rhs_lo(rhs, bt - 2, src)
                    if nxt and bt == 3:
                        split_lo(nxt, 0, 1, chunks=(1,))
                if rhs is not None:
                    rhs_lo(rhs, NBT - 2, src)
                    rhs_lo(rhs, NBT - 1, src)

            dve.memset(u_pad[:, 0:HIST], 0.0).then_inc(zero_ready, 1)
            dve.memset(shift, 0.0).then_inc(zero_ready, 1)
            split_lo(ph["w_in"], 0, 0, chunks=(0,))
            for bt in range(NBT):
                rhs_lo(RHS_X, bt, xr)
                if bt == 0:
                    split_lo(ph["w_in"], 0, 0, chunks=(1,))
                if bt == 1:
                    split_lo(ph["w_in"], 0, 1, chunks=(0,))
                if bt == 3:
                    split_lo(ph["w_in"], 0, 1, chunks=(1,))
            dve.wait_ge(tables_loaded, 32)

            p = ph["w_in"]

            def conv(i, end, first=False):
                split_next(p, i, 0, end)
                dve.wait_ge(bank_read[1], bank_count(p, i))
                dve.scalar_tensor_tensor(u_pad[:, HIST:HIST + T], acc[0][:, 0:T], par("b_in")[:, i, :], work[:, 0, :],
                                         ALU.add, ALU.mult).then_inc(bank_read[0], 1)
                split_next(p, i, 1, end)
                if not first:
                    join(i - 1)
                dve.wait_ge(useg_built, i + 1)
                sums = [b[:, 0:T].rearrange("p (s q) -> p s q", q=SEG) for b in sc]
                w = par("w_dw")[:, i, :]
                steps = DVE_TAPS * i
                dve.tensor_scalar(sums[0], u_seg[:, :, 0:SEG], w[:, 0:1], par("b_dw")[:, i, :], ALU.mult, ALU.add
                                  ).then_inc(dve_taps, 1)
                if not first:
                    dve.wait_ge(shifted, i)
                dve.tensor_scalar(sums[1], u_seg[:, :, 1:1 + SEG], w[:, 1:2], None, ALU.mult).then_inc(dve_taps, 1)
                for tap in range(2, DVE_TAPS):
                    dst = sums[tap % 2]
                    dve.wait_ge(dve_taps, steps + tap - 1)
                    dve.scalar_tensor_tensor(dst, u_seg[:, :, tap:tap + SEG], w[:, tap:tap + 1], dst,
                                             ALU.mult, ALU.add).then_inc(dve_taps, 1)

            def join(i, done=shifted):
                dve.wait_ge(dve_taps, DVE_TAPS * (i + 1))
                dve.wait_ge(pool_taps, POOL_TAPS * (i + 1))
                dve.tensor_tensor(taps_part[:, :], sc[0][:, 0:T], taps_pool[:, :], ALU.add).then_inc(parts_joined, 1)
                dve.wait_ge(parts_joined, i + 1)
                dve.tensor_tensor(conv_y[:, i, :], sc[1][:, 0:T], taps_part[:, :], ALU.add).then_inc(done, 1)

            conv(0, False, first=True)
            join(0, conv0_done)
            dve.wait_ge(shift_ready, 1)
            dve.tensor_scalar(shift, pt[0][:, 0:T], -1.0, None, ALU.mult).then_inc(shift_taken, 1)
            dve.wait_ge(shift_taken, 1)
            dve.tensor_tensor(conv_y[:, 0, :], conv_y[:, 0, :], shift, ALU.add).then_inc(shifted, 1)

            conv(1, False, first=True)
            pairs(p, conv, first=2)
            join(KD - 1)
            norm(0, conv_y, None, RHS_CONV)

            def add_projection(p, ip, par_, scale):
                k = 2 * ip + par_
                dve.wait_ge(multiplied, group_done(p, ip, par_))
                dve.scalar_tensor_tensor(xr[:, k, :], xr[:, k, :], scale, acc[par_][:, 0:T],
                                         ALU.mult, ALU.add).then_inc(bank_read[par_], 1)

            def residual(p, scale, n):
                add_projection(p, 0, 0, scale)
                split_next(p, 0, 0, False)
                add_projection(p, 0, 1, scale)
                split_next(p, 0, 1, False)
                dve.wait_ge(shift_ready, n + 1)
                dve.tensor_copy(shift, st[:, 0:T]).then_inc(shift_taken, 1)
                dve.wait_ge(shift_taken, n + 1)
                dve.tensor_tensor(xr[:, 0:2, :], xr[:, 0:2, :], over_tiles(shift, 2), ALU.subtract
                                  ).then_inc(shifted, 2)
                dve.wait_ge(shifted, KD * n + 2)
                dve.tensor_tensor(acc_sum, xr[:, 0, :], xr[:, 1, :], ALU.add).then_inc(sum_added, 1)
                dve.wait_ge(squared, KD * n + 2)
                dve.tensor_tensor(acc_sq, acc_sq, work[:, 1, :], ALU.add).then_inc(sq_added, 1)

                def body(ip, end):
                    for par_ in range(2):
                        k = 2 * ip + par_
                        add_projection(p, ip, par_, scale)
                        dve.wait_ge(bank_read[par_], bank_count(p, ip))
                        dve.tensor_tensor(xr[:, k, :], xr[:, k, :], shift, ALU.subtract).then_inc(shifted, 1)
                        if end and par_ == 1:
                            if p.name in after:
                                split_lo(after[p.name], 0, 1, chunks=(0,))
                            break
                        split_next(p, ip, par_, end)
                        dve.wait_ge(shifted, KD * n + k + 1)
                        dve.wait_ge(sum_added, (KD - 2) * (n - 1) + k - 1)
                        dve.tensor_tensor(acc_sum, acc_sum, xr[:, k, :], ALU.add).then_inc(sum_added, 1)
                        dve.wait_ge(squared, KD * n + k + 1)
                        dve.wait_ge(sq_added, (KD - 2) * (n - 1) + k - 1)
                        dve.tensor_tensor(acc_sq, acc_sq, work[:, 1, :], ALU.add).then_inc(sq_added, 1)

                pairs(p, body, first=1)

            def residual_only(p, scale):
                def body(ip, end):
                    for par_ in range(2):
                        add_projection(p, ip, par_, scale)
                        split_next(p, ip, par_, end)
                pairs(p, body)

            residual(ph["w_out"], 1.0, 1)
            norm(1, xr, after["w_out"], RHS_MIX0)

            def ffn(l, n_norm, rhs):
                if l:
                    dve.wait_ge(kv_saved, 64)
                else:
                    dve.wait_ge(state_saved, 16 * KD)
                for h in range(2):
                    p = ph[f"up{l}{h}"]

                    def body(i, end):
                        tile = i + KF * l + HALF * h
                        taps = par("f_w_dw")[:, tile, :]
                        gy = work[:, 0, :]
                        gy_s = work[:, 0, SEQ:T].rearrange("p (n q) -> p n q", q=NQ)
                        dve.wait_ge(gate_taken, tile + 1)
                        dve.scalar_tensor_tensor(gy[:, 1:SEQ], acc[0][:, 0:SEQ - 1], taps[:, 1:2], gy[:, 1:SEQ],
                                                 ALU.mult, ALU.add).then_inc(taps_done, 1)
                        dve.scalar_tensor_tensor(gy_s, gate_s[:, :, 1:1 + NQ], taps[:, 1:2], gy_s,
                                                 ALU.mult, ALU.add).then_inc(taps_done, 1)
                        dve.wait_ge(taps_done, 3 * tile + 1)
                        dve.scalar_tensor_tensor(gy[:, 2:SEQ], acc[0][:, 0:SEQ - 2], taps[:, 0:1], gy[:, 2:SEQ],
                                                 ALU.mult, ALU.add).then_inc(taps_done, 1)
                        dve.wait_ge(taps_done, 3 * tile + 2)
                        dve.scalar_tensor_tensor(gy_s, gate_s[:, :, 0:NQ], taps[:, 0:1], gy_s,
                                                 ALU.mult, ALU.add).then_inc(bank_read[0], 1)
                        split_next(p, i, 0, end)
                        dve.wait_ge(multiplied, group_done(p, i, 1))
                        dve.wait_ge(gelu_done, tile + 1)
                        dve.tensor_tensor(work[:, 1, :], gy, acc[1][:, 0:T], ALU.mult).then_inc(bank_read[1], 1)
                        split_next(p, i, 1, end)
                        dve.wait_ge(h_hi_ready, tile + 1)
                        dve.tensor_tensor(hl[:, i, :], work[:, 1, :], hh[:, i, :], ALU.subtract).then_inc(h_ready, 1)

                    pairs(p, body)
                    down = ph[f"down{l}{h}"]
                    if h == 0:
                        residual_only(down, ALPHA)
                    else:
                        residual(down, 1.0, n_norm)
                norm(n_norm, xr, after.get(down.name), rhs)

            ffn(0, 2, RHS_FFN0)

            p = ph["w_kv"]
            for ip, dst in enumerate([k_t, v_t]):
                for par_ in range(2):
                    dve.wait_ge(multiplied, group_done(p, ip, par_))
                    dve.tensor_copy(dst[:, par_, :], acc[par_][:, 0:T]).then_inc(bank_read[par_], 1)
                    split_next(p, ip, par_, ip == 1)

            p = ph["w_q"]

            def softmax_max(pair, par_, a):
                t = 2 * pair + par_
                if not (isinstance(t, int) and t == 0):
                    dve.wait_ge(probs_turned, t)
                dist = const("dist").rearrange("p a b -> p (a b)")
                for r in range(2):
                    dve.wait_ge(scores_ready, 2 * t + r + 1)
                    dve.scalar_tensor_tensor(probs[:, r, :, :].rearrange("p a b -> p (a b)"), dist,
                                             const("negslope")[:, 8 * a + 8 * r + t, :], sc[r][:, 0:3 * P],
                                             ALU.mult, ALU.add).then_inc(scores_read, 1)
                dve.wait_ge(scores_read, 2 * t + 2)
                dve.tensor_reduce(rowmax, probs[:, :, :, :].rearrange("p a b c -> p (a b) c"), AXX, ALU.max
                                  ).then_inc(softmax_step, 1)
                dve.wait_ge(softmax_step, 10 * t + 1)
                rm = rowmax.rearrange("p (r c) -> p r c", c=3)
                dve.tensor_tensor(rm[:, :, 1:2], rm[:, :, 1:2], rm[:, :, 2:3], ALU.max).then_inc(softmax_step, 1)
                dve.wait_ge(softmax_step, 10 * t + 2)
                for r in range(2):
                    dve.tensor_scalar(negmax[:, 2 * r:2 * r + 2], rm[:, r, 0:2], par("sinks")[:, 8 * a + 8 * r + t, :],
                                      -1.0, ALU.max, ALU.mult).then_inc(softmax_step, 1)

            def softmax_divide(pair, par_):
                t = 2 * pair + par_
                dve.wait_ge(exp_done, t + 1)
                dve.tensor_tensor(denom, rowsum, sinkexp, ALU.add).then_inc(softmax_step, 1)
                dve.wait_ge(softmax_step, 10 * t + 5)
                dve.reciprocal(rdenom, denom).then_inc(softmax_step, 1)
                dve.wait_ge(softmax_step, 10 * t + 6)
                for r in range(2):
                    dve.tensor_scalar(probs[:, r, 0, :], probs[:, r, 0, :], rdenom[:, 2 * r:2 * r + 1], None,
                                      ALU.mult).then_inc(softmax_step, 1)
                    dve.tensor_scalar(probs[:, r, 1:3, :], probs[:, r, 1:3, :], rdenom[:, 2 * r + 1:2 * r + 2], None,
                                      ALU.mult).then_inc(softmax_step, 1)

            def take_out(pair, par_):
                t = 2 * pair + par_
                dve.wait_ge(out_ready, t + 1)
                dve.tensor_copy(qo[:, t, 0:SEQ], ot[:, 0:SEQ]).then_inc(out_read, 1)

            def take_q(ip, par_, a):
                dve.wait_ge(multiplied, group_done(p, ip, par_))
                dve.tensor_scalar(q_st[:, par_, :], acc[par_][:, 0:SEQ], QSCALE, None, ALU.mult)
                dve.tensor_scalar(q_s[:, a, :, 2 * ip + par_ - 8 * a, :],
                                  acc[par_][:, SEQ:T].rearrange("p (n q) -> p n q", q=NQ), QSCALE, None, ALU.mult
                                  ).then_inc(bank_read[par_], 1)

            def q_pair(ip, a1, a2, end=False):
                softmax_max(ip - 1, 1, a1)
                split_lo(p, ip, 1)
                softmax_divide(ip - 1, 1)
                take_out(ip - 1, 0)
                take_q(ip, 0, a2)
                softmax_max(ip, 0, a2)
                if not end:
                    split_lo(p, ip + 1, 0)
                else:
                    split_lo(after[p.name], 0, 0)
                softmax_divide(ip, 0)
                take_out(ip - 1, 1)
                take_q(ip, 1, a2)

            take_q(0, 0, 0)
            softmax_max(0, 0, 0)
            split_lo(p, 1, 0)
            softmax_divide(0, 0)
            take_q(0, 1, 0)
            with dve.Fori(1, KD // 4) as ip:
                q_pair(ip, 0, 0)
            q_pair(KD // 4, 0, 1)
            with dve.Fori(KD // 4 + 1, KD // 2 - 1) as ip:
                q_pair(ip, 1, 1)
            last = KD // 2 - 1
            q_pair(last, 1, 1, end=True)
            softmax_max(last, 1, 1)
            split_lo(after[p.name], 0, 1)
            softmax_divide(last, 1)
            take_out(last, 0)
            take_out(last, 1)

            for rd in range(NB // 2):
                if rd == 0:
                    dve.wait_ge(probs_turned, KD)
                else:
                    dve.wait_ge(s_turned, rd)
                for u in range(4):
                    dve.wait_ge(s_scores_ready, 2 * rd + u // 2 + 1)
                    a = u % 2
                    dve.scalar_tensor_tensor(probs_s[:, u, :], const("dist_s"), const("negslope_s")[:, a, :],
                                             sc[u // 2][:, a * SKEYS:(a + 1) * SKEYS], ALU.mult, ALU.add
                                             ).then_inc(s_scores_read, 1)
                dve.wait_ge(s_scores_read, 4 * rd + 4)
                dve.tensor_reduce(rowmax[:, 0:4], probs_s, AXX, ALU.max).then_inc(s_step, 1)
                dve.wait_ge(s_step, 9 * rd + 1)
                for a in range(2):
                    dve.tensor_scalar(negmax[:, a:a + 3:2], rowmax[:, a:a + 3:2], par("sinks_s")[:, a, :], -1.0,
                                      ALU.max, ALU.mult).then_inc(s_step, 1)
                dve.wait_ge(s_exp_done, rd + 1)
                dve.tensor_tensor(denom, rowsum, sinkexp, ALU.add).then_inc(s_step, 1)
                dve.wait_ge(s_step, 9 * rd + 4)
                dve.reciprocal(rdenom, denom).then_inc(s_step, 1)
                dve.wait_ge(s_step, 9 * rd + 5)
                for u in range(4):
                    dve.tensor_scalar(probs_s[:, u, :], probs_s[:, u, :], rdenom[:, u:u + 1], None, ALU.mult
                                      ).then_inc(s_step, 1)
                dve.wait_ge(s_out_ready, rd + 1)
                for x in range(2):
                    n = 2 * rd + x
                    dve.tensor_copy(qo[:, :, SEQ + n * NQ:SEQ + (n + 1) * NQ],
                                    ot[:, x * P:(x + 1) * P].rearrange("p (t q) -> p t q", q=NQ)
                                    ).then_inc(s_out_read, 1)

            for bt in range(NBT):
                rhs_lo(RHS_ATTN, bt, qo)
            residual(ph["w_o"], ALPHA, 3)
            norm(3, xr, after["w_o"], RHS_MIX1)
            ffn(1, 4, None)



_OUT = {
    "y": (P, KD, T),
    "conv_state_out": (P, KD, NB + 1, HIST),
    "ffn_state_out": (LAYERS, P, KF, NB + 1, FW - 1),
    "k_new": (P, 2, T),
    "v_new": (P, 2, T),
    "kc_out": (NB, WINDOW - NQ, 4 * HD),
    "vc_out": (NB, WINDOW - NQ, 4 * HD),
}


def _stream(w):
    k, n = w.shape
    return w.reshape(k // P, P, n // P, P).transpose(2, 1, 0, 3).reshape(n // P, P, k)


def _feature_tiles(v):
    v = v.reshape(v.shape[:-1] + (v.shape[-1] // P, P))
    return np.moveaxis(np.moveaxis(v, -1, 0), -1, 1)


def _pack(table, values):
    cols = []
    for name, shape in table:
        v = np.asarray(values[name], np.float32)
        cols.append(np.broadcast_to(v, (P,) + v.shape[1:]).reshape(P, -1))
    return np.concatenate(cols, axis=1)


def _constants():
    row = np.arange(P, dtype=np.float32)[:, None]
    col = np.arange(P, dtype=np.float32)[None, :]
    own = np.where(row >= col, row - col, MASKED)
    before = np.where(col >= row, WINDOW + row - col, MASKED)
    q = (np.arange(P) % NQ).astype(np.float32)[:, None]
    key = np.arange(SKEYS, dtype=np.float32)[None, :]
    d = WINDOW + q - key
    slopes = np.float32(2.0) ** (np.float32(-8.0) * np.arange(1, NH + 1, dtype=np.float32) / np.float32(NH))
    return {
        "ident": np.eye(P), "ones_mean": np.full((P, P), 1.0 / D),
        "ones_tile": np.full((P, P), 1.0 / P), "dist": np.stack([own, before, own], axis=1),
        "dist_s": np.where((d >= 0) & (d <= WINDOW), d, MASKED),
        "eps": np.full((P, 1), EPS), "negslope": -slopes[None, :, None],
        "negslope_s": -np.repeat(slopes.reshape(2, 2 * 8), NQ, axis=1).T[:, :, None],
    }


def kernel(**inputs):
    import concourse.bacc as _bacc
    from concourse.bass_utils import run_bass_kernel_spmd as _run

    a = {k: np.asarray(v) for k, v in inputs.items()}
    tokens = np.concatenate([a["x_prompt"].reshape(SEQ, D), a["x_sample"].reshape(NS, D)])
    wq = a["b_w_q"][0].reshape(D, 2, 2, 8, HD).transpose(0, 1, 3, 2, 4).reshape(D, D)
    wo = a["b_w_o"][0].reshape(2, 2, 8, HD, D).transpose(0, 2, 1, 3, 4).reshape(D, D)

    arrays = {"x": _feature_tiles(tokens.T[None].transpose(0, 2, 1))[:, :, 0]}
    w_in = _stream(a["a_w_in"][0])
    arrays["w_in"] = w_in.reshape(2, KD, P, D).transpose(1, 0, 2, 3).reshape(2 * KD, P, D)
    arrays["w_out"] = _stream(a["a_w_out"][0])
    arrays["w_kv"], arrays["w_q"], arrays["w_o"] = _stream(a["w_kv"]), _stream(wq), _stream(wo)
    for l in range(LAYERS):
        up = _stream(a["f_w_up"][l]).reshape(2, KF, P, D)
        for h in range(2):
            part = slice(h * HALF, (h + 1) * HALF)
            arrays[f"up{l}{h}"] = up[:, part].transpose(1, 0, 2, 3).reshape(2 * HALF, P, D)
            arrays[f"down{l}{h}"] = _stream(a["f_w_down"][l][h * HALF * P:(h + 1) * HALF * P])
    arrays["conv_state"] = _feature_tiles(a["state_conv_a"][0])
    arrays["ffn_state"] = np.stack([_feature_tiles(s) for s in a["state_ffn_conv"]])
    kc = a["cache_k_win"].reshape(NB, WINDOW, 2, P)
    arrays["k_cache_t"] = kc.transpose(3, 2, 0, 1)
    arrays["k_cache"] = a["cache_k_win"].reshape(NB, WINDOW, 4 * HD)
    arrays["v_cache"] = a["cache_v_win"].reshape(NB, WINDOW, 4 * HD)

    def per_layer(v):
        v = np.stack([_feature_tiles(x) for x in v], axis=1)
        return v.reshape(P, -1, 1)

    sinks = a["b_sinks"][0]
    arrays["params"] = _pack(PARAMS, {
        "b_in": _feature_tiles(a["a_b_in"][0])[:, :, None], "w_dw": _feature_tiles(a["a_w_dw"][0]),
        "b_dw": _feature_tiles(a["a_b_dw"][0])[:, :, None], "norm_g": _feature_tiles(a["a_norm_g"][0])[:, :, None],
        "norm_b": _feature_tiles(a["a_norm_b"][0])[:, :, None], "b_out": _feature_tiles(a["a_b_out"][0])[:, :, None],
        "f_w_dw": np.concatenate([_feature_tiles(x) for x in a["f_w_dw"]], axis=1),
        "f_b_dw": per_layer(a["f_b_dw"]), "mix_g": per_layer(a["ln_mix_g"]), "mix_b": per_layer(a["ln_mix_b"]),
        "ffn_g": per_layer(a["ln_ffn_g"]), "ffn_b": per_layer(a["ln_ffn_b"]),
        "sinks": sinks[None, :, None],
        "sinks_s": np.repeat(sinks.reshape(2, 2 * 8), NQ, axis=1).T[:, :, None],
    })
    arrays["consts"] = _pack(CONSTS, _constants())

    nc = _bacc.Bacc("TRN2", target_bir_lowering=False, num_devices=1)
    io, feed = {}, {}
    for name, v in arrays.items():
        v = np.ascontiguousarray(v)
        feed[f"in_{name}"] = v
        io[name] = nc.dram_tensor(f"in_{name}", v.shape, F32, kind="ExternalInput").ap()
    for name, shape in _OUT.items():
        io[name] = nc.dram_tensor(f"out_{name}", shape, F32, kind="ExternalOutput").ap()
    trunk_kernel(nc, io)
    got = _run(nc, [feed], core_ids=[0]).results[0]
    o = {name: got[f"out_{name}"] for name in _OUT}

    def tokens_of(v):
        v = np.moveaxis(np.moveaxis(v, 1, -1), 0, -1)
        return v.reshape(v.shape[:-2] + (-1,))

    y = tokens_of(o["y"])
    conv = tokens_of(o["conv_state_out"])
    ffn = np.stack([tokens_of(v) for v in o["ffn_state_out"]])
    new = [tokens_of(o["k_new"]), tokens_of(o["v_new"])]
    win_p = [v[SEQ - WINDOW:SEQ].reshape(1, WINDOW, 4, HD) for v in new]
    win_s = [np.concatenate([old, v[SEQ:].reshape(NB, NQ, 4 * HD)], axis=1).reshape(NB, WINDOW, 4, HD)
             for old, v in zip([o["kc_out"], o["vc_out"]], new)]
    return (y[:SEQ].reshape(1, SEQ, D), y[SEQ:].reshape(NB, NQ, D), conv[None, 0:1], ffn[:, 0:1],
            win_p[0], win_p[1], conv[None, 1:], ffn[:, 1:], win_s[0], win_s[1])
```

```python
from contextlib import ExitStack, nullcontext
from collections import namedtuple

import numpy as np

import concourse.bass as bass
from concourse import mybir

F32 = mybir.dt.float32
F32R = mybir.dt.float32r
ALU = mybir.AluOpType
ACT = mybir.ActivationFunctionType
AXX = mybir.AxisListType.X

P = 128
D = 2048
KD = D // P
SEQ = 256
NB, NQ = 8, 8
NS = NB * NQ
T = SEQ + NS
DFF = 5632
KF = DFF // P
HALF = KF // 2
LAYERS = 2
CW = 31
HIST = CW - 1
FW = 3
SEG = 8
NSEG = T // SEG
PSEG = SEQ // SEG
SEGW = HIST + SEG
HD = 64
NH = 32
WINDOW = 128
SKEYS = WINDOW + NQ
ALPHA = float((2.0 * LAYERS) ** 0.25)
EPS = 1e-5
QSCALE = float(HD ** -0.5)
BATCHES = [(0, 1), (1, 2), (2, 4), (4, 8), (8, 12), (12, 16)]
NBT = len(BATCHES)
VECTOR_CENTERS = 3
POOL_TAPS = 13
DVE_TAPS = CW - POOL_TAPS
MASKED = 1e35

Phase = namedtuple("Phase", "name base groups kt")


def phases():
    out, base = {}, 0
    order = [("w_in", 2 * KD, 8), ("w_out", KD, 8)]
    for l in range(LAYERS):
        if l == 1:
            order += [("w_kv", 4, 8), ("w_q", KD, 8), ("w_o", KD, 8)]
        for h in range(2):
            order += [(f"up{l}{h}", 2 * HALF, 8), (f"down{l}{h}", KD, HALF // 2)]
    for name, groups, kt in order:
        out[name] = Phase(name, base, groups, kt)
        base += groups
    return out


PARAMS = [("b_in", (2 * KD, 1)), ("w_dw", (KD, CW)), ("b_dw", (KD, 1)), ("norm_g", (KD, 1)), ("norm_b", (KD, 1)),
          ("b_out", (KD, 1)), ("f_w_dw", (LAYERS * KF, FW)), ("f_b_dw", (LAYERS * KF, 1)),
          ("mix_g", (LAYERS * KD, 1)), ("mix_b", (LAYERS * KD, 1)), ("ffn_g", (LAYERS * KD, 1)),
          ("ffn_b", (LAYERS * KD, 1)), ("sinks", (NH, 1)), ("sinks_s", (2, 1))]
CONSTS = [("ident", (P,)), ("ones_mean", (P,)), ("ones_tile", (P,)), ("dist", (3, P)), ("dist_s", (SKEYS,)),
          ("negslope", (NH, 1)), ("negslope_s", (2, 1)), ("eps", (1,))]


def columns(table):
    at, out = 0, {}
    for name, shape in table:
        n = int(np.prod(shape))
        out[name] = (at, n, shape)
        at += n
    return out, at


def trunk_kernel(nc, io):
    ph = phases()
    pcols, n_params = columns(PARAMS)
    ccols, n_consts = columns(CONSTS)

    with ExitStack() as ctx:
        def sb(name, shape, dt=F32):
            return ctx.enter_context(nc.sbuf_tensor(name, shape, dt))

        def sem(name):
            return ctx.enter_context(nc.semaphore(name))

        def bank(name):
            return ctx.enter_context(nc.psum_tensor(name, [P, 512], F32))

        xr = sb("xr", [P, KD, T])
        xh = sb("xh", [P, KD, T], F32R)
        xl = sb("xl", [P, KD, T], F32R)
        CHUNK = HALF // 2 * P
        w_raw = sb("w_raw", [P, 4, CHUNK])
        w_hi = sb("w_hi", [P, 4, CHUNK], F32R)
        w_lo = sb("w_lo", [P, 4, CHUNK], F32R)
        params = sb("params", [P, n_params])
        consts = sb("consts", [P, n_consts])
        work = sb("work", [P, 2, T])
        rows4 = sb("rows4", [P, 4, T])
        acc_sum, acc_sq, shift, rstd = (rows4[:, i, :] for i in range(4))
        probs_t = rows4[:, :, :].rearrange("p a b -> p (a b)")[:, 0:6 * P]
        ffn_in = sb("ffn_in", [P, KF, NB, FW - 1])
        ffn_out = sb("ffn_out", [P, KF, NB + 1, FW - 1])
        gate_s = sb("gate_s", [P, NB, FW - 1 + NQ])
        with nc.sbuf_tensor("conv_y", [P, KD, T], F32) as conv_y, \
                nc.sbuf_tensor("u_pad", [P, HIST + T], F32) as u_pad, \
                nc.sbuf_tensor("u_seg", [P, NSEG, SEGW], F32) as u_seg, \
                nc.sbuf_tensor("hist", [P, KD, NB, HIST], F32) as hist, \
                nc.sbuf_tensor("prods", [P, POOL_TAPS, T], F32) as prods, \
                nc.sbuf_tensor("taps_pool", [P, T], F32) as taps_pool:
            pass
        with nc.sbuf_tensor("k_t", [P, 2, T], F32) as k_t, \
                nc.sbuf_tensor("kc_t", [P, 2, NB, WINDOW], F32) as kc_t, \
                nc.sbuf_tensor("v_c", [P, NB, 4 * HD], F32) as v_c, \
                nc.sbuf_tensor("v_p", [P, 2, 4 * HD], F32) as v_p, \
                nc.sbuf_tensor("v_n", [P, NB, 4 * HD], F32) as v_n, \
                nc.sbuf_tensor("qo", [P, KD, T], F32) as qo, \
                nc.sbuf_tensor("q_st", [P, 2, SEQ], F32) as q_st, \
                nc.sbuf_tensor("q_s", [P, 2, NB, 8, NQ], F32) as q_s, \
                nc.sbuf_tensor("probs", [P, 2, 3, P], F32) as probs, \
                nc.sbuf_tensor("smx", [P, 6, 6], F32) as smx:
            pass
        hh = sb("hh", [P, HALF, T], F32R)
        hl = sb("hl", [P, HALF, T], F32R)

        acc = [bank("acc0"), bank("acc1")]
        sc = [bank("sc0"), bank("sc1")]
        pt = [bank("pt0"), bank("pt1")]
        ot = bank("ot")
        st = bank("st")

        def par(name):
            a, n, shape = pcols[name]
            return params[:, a:a + n].rearrange("p (i t) -> p i t", t=shape[1])

        def const(name):
            a, n, shape = ccols[name]
            v = consts[:, a:a + n]
            return v.rearrange("p (i t) -> p i t", t=shape[1]) if len(shape) == 2 else v

        ident, ones_mean, ones_tile = const("ident"), const("ones_mean"), const("ones_tile")
        v_t = work[:, :, :]
        probs_s = [v[:, 0:4 * SKEYS].rearrange("p (u k) -> p u k", u=4) for v in (
            probs[:, :, :, :].rearrange("p a b c -> p (a b c)"), ffn_out[:, :, :, :].rearrange("p a b c -> p (a b c)"))]
        probs_tn = work[:, :, :].rearrange("p a b -> p (a b)")
        rowmax, negmax = smx[:, 0, :], smx[:, 1, 0:4]
        rowsum, sinkexp = smx[:, 2, 0:4], smx[:, 3, 0:4]
        denom, rdenom = smx[:, 4, 0:4], smx[:, 5, 0:4]

        raw_loaded = [sem(f"raw_loaded{s}") for s in range(4)]
        hi_ready, lo_ready = sem("hi_ready"), sem("lo_ready")
        multiplied = sem("multiplied")
        bank_read = [sem("bank_read0"), sem("bank_read1")]
        x_loaded = [sem(f"x_loaded{b}") for b in range(NBT)]
        tables_loaded = sem("tables_loaded")
        rhs_hi_ready, rhs_ready = sem("rhs_hi_ready"), sem("rhs_ready")
        zero_ready = sem("zero_ready")
        hist_loaded, state_saved, useg_built = sem("hist_loaded"), sem("state_saved"), sem("useg_built")
        prod_ready, parts_joined = sem("prod_ready"), sem("parts_joined")
        products_summed, sum_taken = sem("products_summed"), sem("sum_taken")
        dve_taps, pool_taps, conv0_done = sem("dve_taps"), sem("pool_taps"), sem("conv0_done")
        shift_ready, shift_taken, shifted = sem("shift_ready"), sem("shift_taken"), sem("shifted")
        squared, square_added = sem("squared"), sem("square_added")
        sum_added, sq_added = sem("sum_added"), sem("sq_added")
        mean_taken, pool_centered = sem("mean_taken"), sem("pool_centered")
        mean_ready, mean_squared, moments_ready = sem("mean_ready"), sem("mean_squared"), sem("moments_ready")
        var_ready, std_ready, rstd_ready = sem("var_ready"), sem("std_ready"), sem("rstd_ready")
        centered, scaled, applied = sem("centered"), sem("scaled"), sem("applied")
        ffn_in_loaded, ffn_out_saved = sem("ffn_in_loaded"), sem("ffn_out_saved")
        gate_taken, taps_done, gelu_done = sem("gate_taken"), sem("taps_done"), sem("gelu_done")
        h_hi_ready, h_ready = sem("h_hi_ready"), sem("h_ready")
        cache_loaded, kv_saved = sem("cache_loaded"), sem("kv_saved")
        v_transposed, v_taken = sem("v_transposed"), sem("v_taken")
        scores_ready, scores_read, softmax_step = sem("scores_ready"), sem("scores_read"), sem("softmax_step")
        exp_done, probs_turned, probs_taken = sem("exp_done"), sem("probs_turned"), sem("probs_taken")
        out_ready, out_read = sem("out_ready"), sem("out_read")
        s_scores_ready, s_scores_read, s_step = sem("s_scores_ready"), sem("s_scores_read"), sem("s_step")
        s_exp_done, s_turned, s_taken = sem("s_exp_done"), sem("s_turned"), sem("s_taken")
        s_out_ready, s_out_read = sem("s_out_ready"), sem("s_out_read")
        last_applied, y_saved = sem("last_applied"), sem("y_saved")

        def chunk(p, ip, par_, j):
            return 2 * p.base + 4 * ip + 2 * par_ + j

        def splits(p, ip, par_, j):
            if p.base == 0 and isinstance(ip, int) and ip == 0:
                return 2 * j + par_ + 1
            return chunk(p, ip, par_, j) + 1

        def group_done(p, ip, par_):
            return chunk(p, ip, par_, 0) + 2

        def bank_count(p, ip):
            return p.base // 2 + ip + 1

        RHS_X, RHS_CONV, RHS_MIX0, RHS_FFN0, RHS_ATTN, RHS_MIX1 = (NBT * e for e in range(6))

        def over_tiles(row, n):
            return bass.AP(row.tensor, row.offset, [row.ap[0], [0, n], [1, T]])

        order = list(ph.values())
        after = {a.name: b for a, b in zip(order, order[1:])}

        block = ctx.enter_context(nc.Block())

        @block.sync
        def _(sp):
            def load(p, ip, par_, wait=True, chunks=(0, 1)):
                for j in chunks:
                    slot, n = 2 * par_ + j, p.kt * P
                    if wait:
                        sp.wait_ge(lo_ready, splits(p, ip - 1, par_, j) if p.base == 0 and isinstance(ip, int)
                                   else chunk(p, ip, par_, j) - 3)
                    sp.dma_start(w_raw[:, slot, 0:n], io[p.name][2 * ip + par_, :, j * n:(j + 1) * n]
                                 ).then_inc(raw_loaded[slot], 16)

            for p in order:
                first = 0
                if p.base == 0:
                    def load_x(b):
                        lo, hi = BATCHES[b]
                        sp.dma_start(xr[:, lo:hi, :], io["x"][:, lo:hi, :]).then_inc(x_loaded[b], 16)

                    load(p, 0, 0, wait=False, chunks=(0,))
                    load_x(0)
                    load(p, 0, 1, wait=False, chunks=(0,))
                    for b in range(1, NBT - 2):
                        load_x(b)
                    load(p, 0, 0, wait=False, chunks=(1,))
                    load_x(NBT - 2)
                    load(p, 0, 1, wait=False, chunks=(1,))
                    load_x(NBT - 1)
                    first = 2
                    load(p, 1, 0)
                    sp.dma_start(params[:, :], io["params"]).then_inc(tables_loaded, 16)
                    sp.dma_start(consts[:, :], io["consts"]).then_inc(tables_loaded, 16)
                    sp.dma_start(hist[:, 0, :, :], io["conv_state"][:, 0]).then_inc(hist_loaded, 16)
                    load(p, 1, 1)
                    sp.dma_start(hist[:, 1:KD, :, :], io["conv_state"][:, 1:KD]).then_inc(hist_loaded, 16)
                with sp.Fori(first, p.groups // 2) as ip:
                    load(p, ip, 0)
                    load(p, ip, 1)
            for lo, hi in BATCHES[2:]:
                lo = 0 if lo == 2 else lo
                if hi < KD:
                    sp.wait_ge(applied, 4 * KD + hi)
                else:
                    sp.wait_ge(last_applied, hi - lo)
                sp.dma_start(io["y"][:, lo:hi, :], xr[:, lo:hi, :]).then_inc(y_saved, 16)
            sp.wait_ge(y_saved, 16 * (NBT - 2))

        @block.gpsimd
        def _(pool):
            def conv_taps(i, first=False):
                if not first:
                    pool.wait_ge(shift_taken, 1)
                    pool.wait_ge(shifted, i)
                for n in range(POOL_TAPS):
                    pool.wait_ge(prod_ready, POOL_TAPS * i + n + 1)
                    if n:
                        pool.wait_ge(pool_taps, POOL_TAPS * i + n)
                    pool.tensor_tensor(taps_pool[:, :], prods[:, n, :], taps_pool[:, :] if n else shift, ALU.add
                                       ).then_inc(pool_taps, 1)

            pool.wait_ge(zero_ready, 2)
            conv_taps(0, first=True)
            pool.dma_start(ffn_in[:, :, :, :], io["ffn_state"][0]).then_inc(ffn_in_loaded, 16)
            pool.dma_start(io["kc_out"], io["k_cache"][:, NQ:WINDOW, :]).then_inc(kv_saved, 16)
            pool.dma_start(io["vc_out"], io["v_cache"][:, NQ:WINDOW, :]).then_inc(kv_saved, 16)
            with pool.Fori(1, KD - 1) as i:
                conv_taps(i)

            def center(n, src):
                pool.wait_ge(mean_taken, n + 1)
                for lo, hi in BATCHES[VECTOR_CENTERS:]:
                    pool.tensor_tensor(src[:, lo:hi, :], src[:, lo:hi, :], over_tiles(shift, hi - lo), ALU.subtract
                                       ).then_inc(pool_centered, 1)

            center(0, conv_y)
            center(1, xr)

            pool.wait_ge(h_ready, KF)
            pool.dma_start(io["ffn_state_out"][0], ffn_out[:, :, :, :]).then_inc(ffn_out_saved, 16)
            pool.dma_start(ffn_in[:, :, :, :], io["ffn_state"][1]).then_inc(ffn_in_loaded, 16)
            center(2, xr)
            pool.wait_ge(multiplied, 2 * ph["w_kv"].base)
            pool.dma_start(kc_t[:, :, :, :], io["k_cache_t"]).then_inc(cache_loaded, 16)
            pool.dma_start(v_c[:, :, :], io["v_cache"].rearrange("n k c -> k n c")).then_inc(cache_loaded, 16)
            pool.wait_ge(bank_read[0], bank_count(ph["w_kv"], 1))
            pool.wait_ge(bank_read[1], bank_count(ph["w_kv"], 1))
            pool.dma_start(io["k_new"], k_t[:, :, :]).then_inc(kv_saved, 16)
            pool.dma_start(io["v_new"], v_t).then_inc(kv_saved, 16)
            center(3, xr)
            pool.wait_ge(h_ready, 2 * KF)
            pool.dma_start(io["ffn_state_out"][1], ffn_out[:, :, :, :]).then_inc(ffn_out_saved, 16)
            center(4, xr)
            pool.wait_ge(state_saved, 16 * KD)
            pool.wait_ge(kv_saved, 64)
            pool.wait_ge(ffn_out_saved, 32)

        @block.tensor
        def _(pe):
            def project_chunk(p, ip, par_, j, hi, lo, rhs_wait=None):
                slot = 2 * par_ + j
                if j == 0 and not (p.base == 0 and isinstance(ip, int) and ip == 0):
                    pe.wait_ge(bank_read[par_], bank_count(p, ip) - 1)
                pe.wait_ge(lo_ready, splits(p, ip, par_, j))
                for i in range(p.kt):
                    k = j * p.kt + i
                    if rhs_wait is not None:
                        pe.wait_ge(rhs_wait[0], rhs_wait[1] + k + 1)
                    wh, wl = w_hi[:, slot, i * P:(i + 1) * P], w_lo[:, slot, i * P:(i + 1) * P]
                    out = acc[par_][:, 0:T]
                    first, last = k == 0, k == 2 * p.kt - 1
                    pe.matmul(out, wh, hi[:, k, :], start=first, stop=False)
                    pe.matmul(out, wh, lo[:, k, :], start=False, stop=False)
                    mm = pe.matmul(out, wl, hi[:, k, :], start=False, stop=last)
                mm.then_inc(multiplied, 1)

            def project_group(p, ip, par_, hi, lo, rhs_wait=None):
                for j in range(2):
                    project_chunk(p, ip, par_, j, hi, lo, rhs_wait)

            def project_first_pair(p, hi, lo, event):
                for par_ in range(2):
                    if p.base:
                        pe.wait_ge(bank_read[par_], bank_count(p, 0) - 1)
                for b, (first, end) in enumerate(BATCHES):
                    pe.wait_ge(rhs_ready, event + b + 1)
                    for par_ in range(2):
                        for k in range(first, end):
                            j, i = k // p.kt, k % p.kt
                            if i == 0:
                                pe.wait_ge(lo_ready, splits(p, 0, par_, j))
                            slot = 2 * par_ + j
                            wh, wl = w_hi[:, slot, i * P:(i + 1) * P], w_lo[:, slot, i * P:(i + 1) * P]
                            out = acc[par_][:, 0:T]
                            pe.matmul(out, wh, hi[:, k, :], start=(k == 0), stop=False)
                            pe.matmul(out, wh, lo[:, k, :], start=False, stop=False)
                            mm = pe.matmul(out, wl, hi[:, k, :], start=False, stop=(k == KD - 1))
                            if i == p.kt - 1:
                                n = {(0, 0): 1, (1, 0): 0, (0, 1): 2, (1, 1): 1}[(par_, j)]
                                if n:
                                    mm.then_inc(multiplied, n)

            def project_pairs(p, hi, lo, last=None):
                with pe.Fori(1, p.groups // 2 - (last is not None)) as ip:
                    project_group(p, ip, 0, hi, lo)
                    project_group(p, ip, 1, hi, lo)
                if last is not None:
                    ip = p.groups // 2 - 1
                    project_group(p, ip, 0, hi, lo)
                    project_chunk(p, ip, 1, 0, hi, lo)
                    last()
                    project_chunk(p, ip, 1, 1, hi, lo)

            def project(p, hi, lo, rhs_wait):
                project_group(p, 0, 0, hi, lo, rhs_wait)
                project_group(p, 0, 1, hi, lo)
                project_pairs(p, hi, lo)

            def find_shift(p, n):
                pe.wait_ge(bank_read[0], bank_count(p, 0))
                pe.matmul(st[:, 0:T], ones_tile, xr[:, 0, :], start=True, stop=True).then_inc(shift_ready, 1)

            def project_residual(p, hi, lo, n, event=None, rhs_wait=None):
                if event is None:
                    project_group(p, 0, 0, hi, lo, rhs_wait)
                    project_group(p, 0, 1, hi, lo)
                else:
                    project_first_pair(p, hi, lo, event)
                find_shift(p, n)

                def sum_moments():
                    pe.wait_ge(sum_added, (KD - 2) * n)
                    pe.wait_ge(shift_taken, n + 1)
                    pe.matmul(st[:, 0:T], ones_mean, acc_sum, start=True, stop=False)
                    pe.wait_ge(sq_added, (KD - 2) * n)
                    pe.matmul(ot[:, 0:T], ones_mean, acc_sq, start=True, stop=False)

                project_pairs(p, hi, lo, last=sum_moments)
                pe.wait_ge(bank_read[1], bank_count(p, p.groups // 2 - 1))
                pe.matmul(st[:, 0:T], ones_mean, xr[:, KD - 1, :], start=False, stop=True).then_inc(mean_ready, 1)
                pe.wait_ge(squared, KD * (n + 1))
                pe.matmul(ot[:, 0:T], ones_mean, work[:, 1, :], start=False, stop=True).then_inc(moments_ready, 1)

            p = ph["w_in"]

            def add_moments(i, between=None):
                first, last = isinstance(i, int) and i == 0, isinstance(i, int) and i == KD - 1
                pe.wait_ge(shifted, i + 1)
                mm = pe.matmul(st[:, 0:T], ones_mean, conv_y[:, i, :], start=first, stop=last)
                if last:
                    mm.then_inc(mean_ready, 1)
                if between:
                    between()
                pe.wait_ge(squared, i + 1)
                pe.matmul(ot[:, 0:T], ones_mean, work[:, 1, :], start=first, stop=last).then_inc(
                    moments_ready if last else square_added, 1)

            project_first_pair(p, xh, xl, RHS_X)
            project_group(p, 1, 0, xh, xl)
            project_group(p, 1, 1, xh, xl)
            project_chunk(p, 2, 0, 0, xh, xl)
            pe.wait_ge(tables_loaded, 32)
            pe.wait_ge(conv0_done, 1)
            pe.matmul(pt[0][:, 0:T], ones_tile, conv_y[:, 0, :], start=True, stop=True).then_inc(shift_ready, 1)
            project_chunk(p, 2, 0, 1, xh, xl)
            project_group(p, 2, 1, xh, xl)
            add_moments(0)
            with pe.Fori(3, KD) as ip:
                project_group(p, ip, 0, xh, xl)
                project_group(p, ip, 1, xh, xl)
                add_moments(ip - 2)

            def sum_products():
                pe.matmul(pt[0][:, 0:T], ident, shift, start=True, stop=False)
                for n in range(POOL_TAPS):
                    pe.wait_ge(prod_ready, POOL_TAPS * (KD - 1) + n + 1)
                    pe.matmul(pt[0][:, 0:T], ident, prods[:, n, :], start=False,
                              stop=(n == POOL_TAPS - 1)).then_inc(products_summed, 1)

            add_moments(KD - 2, between=sum_products)
            add_moments(KD - 1)
            project_residual(ph["w_out"], xh, xl, 1, event=RHS_CONV)

            def ffn(l, event):
                for h in range(2):
                    up, down = ph[f"up{l}{h}"], ph[f"down{l}{h}"]
                    if h == 0:
                        project_first_pair(up, xh, xl, event)
                        project_pairs(up, xh, xl)
                        project(down, hh, hl, (h_ready, KF * l))
                    else:
                        project(up, xh, xl, None)
                        project_residual(down, hh, hl, 2 * l + 2, rhs_wait=(h_ready, KF * l + HALF))

            ffn(0, RHS_MIX0)

            p = ph["w_kv"]
            project_first_pair(p, xh, xl, RHS_FFN0)
            project_group(p, 1, 0, xh, xl)
            project_group(p, 1, 1, xh, xl)

            p = ph["w_q"]

            def turn_v():
                pe.wait_ge(bank_read[0], bank_count(ph["w_kv"], 1))
                pe.wait_ge(bank_read[1], bank_count(ph["w_kv"], 1))
                for b in range(2):
                    for a in range(2):
                        pe.transpose(pt[0][:, b * 256 + a * P:b * 256 + (a + 1) * P],
                                     v_t[:, a, b * P:(b + 1) * P], ident)
                for n in range(NB):
                    dst = [sc[0], sc[1], pt[1], ot][n // 2]
                    for a in range(2):
                        tr = pe.transpose(dst[0:NQ, (n % 2) * 256 + a * P:(n % 2) * 256 + (a + 1) * P],
                                          v_t[:, a, SEQ + n * NQ:SEQ + (n + 1) * NQ], ident)
                tr.then_inc(v_transposed, 1)

            def scores(pair, par_, a, first=False):
                t = 2 * pair + par_
                pe.wait_ge(bank_read[par_], bank_count(p, pair))
                if first:
                    pe.wait_ge(v_taken, 1)
                else:
                    pe.wait_ge(scores_read, 2 * t)
                for r in range(2):
                    rows = slice(HD * r, HD * r + HD)
                    pe.matmul(sc[r][:, 0:P], q_st[rows, par_, 0:P], k_t[rows, a, 0:P], start=True, stop=True)
                    pe.matmul(sc[r][:, P:3 * P], q_st[rows, par_, P:2 * P], k_t[rows, a, 0:2 * P],
                              start=True, stop=True).then_inc(scores_ready, 1)

            def turn_probs(pair, par_):
                t = 2 * pair + par_
                pe.wait_ge(softmax_step, 10 * t + 10)
                for r in range(2):
                    for c in range(3):
                        tr = pe.transpose(pt[r][:, c * P:(c + 1) * P], probs[:, r, c, :], ident)
                tr.then_inc(probs_turned, 1)

            def weigh_values(pair, par_, a, first=False):
                t = 2 * pair + par_
                pe.wait_ge(probs_taken, t + 1)
                if not first:
                    pe.wait_ge(out_read, t)
                for r in range(2):
                    rows, head = slice(HD * r, HD * r + HD), slice((2 * a + r) * HD, (2 * a + r + 1) * HD)
                    pr = [probs_t[:, (3 * r + c) * P:(3 * r + c + 1) * P] for c in range(3)]
                    pe.matmul(ot[rows, 0:P], v_p[:, 0, head], pr[0], start=True, stop=True)
                    pe.matmul(ot[rows, P:2 * P], v_p[:, 0, head], pr[1], start=True, stop=False)
                    mm = pe.matmul(ot[rows, P:2 * P], v_p[:, 1, head], pr[2], start=False, stop=True)
                mm.then_inc(out_ready, 1)

            def q_pair(ip, a1, a2):
                scores(ip - 1, 1, a1)
                project_chunk(p, ip, 0, 0, xh, xl)
                weigh_values(ip - 1, 0, a1, first=isinstance(ip, int) and ip == 1)
                project_chunk(p, ip, 0, 1, xh, xl)
                turn_probs(ip - 1, 1)
                scores(ip, 0, a2)
                project_chunk(p, ip, 1, 0, xh, xl)
                weigh_values(ip - 1, 1, a1)
                project_chunk(p, ip, 1, 1, xh, xl)
                turn_probs(ip, 0)

            def sample_scores(rd, x):
                if rd:
                    pe.wait_ge(s_scores_read, 4 * (rd - 1) + 2 * (x + 1))
                n = 2 * rd + x
                new = slice(SEQ + n * NQ, SEQ + (n + 1) * NQ)
                for a in range(2):
                    for half in range(2):
                        rows = slice(HD * half, HD * half + HD)
                        q = q_s[rows, a, n, :, :].rearrange("p g q -> p (g q)")
                        pe.matmul(sc[x][rows, a * SKEYS:a * SKEYS + WINDOW], q, kc_t[rows, a, n, :],
                                  start=True, stop=True)
                        mm = pe.matmul(sc[x][rows, a * SKEYS + WINDOW:(a + 1) * SKEYS], q, k_t[rows, a, new],
                                       start=True, stop=True)
                mm.then_inc(s_scores_ready, 1)

            project_chunk(p, 0, 0, 0, xh, xl)
            turn_v()
            project_chunk(p, 0, 0, 1, xh, xl)
            scores(0, 0, 0, first=True)
            project_group(p, 0, 1, xh, xl)
            turn_probs(0, 0)
            with pe.Fori(1, KD // 4) as ip:
                q_pair(ip, 0, 0)
            q_pair(KD // 4, 0, 1)
            with pe.Fori(KD // 4 + 1, KD // 2) as ip:
                q_pair(ip, 1, 1)
            last = KD // 2 - 1
            scores(last, 1, 1)
            weigh_values(last, 0, 1)
            pe.wait_ge(bank_read[0], bank_count(p, last))
            pe.wait_ge(bank_read[1], bank_count(p, last))
            pe.wait_ge(scores_read, 2 * KD)
            pe.wait_ge(cache_loaded, 32)
            for x in range(2):
                sample_scores(0, x)
            turn_probs(last, 1)
            weigh_values(last, 1, 1)

            for rd in range(NB // 2):
                if rd + 1 < NB // 2:
                    sample_scores(rd + 1, 0)
                pe.wait_ge(s_step, 9 * rd + 9)
                if rd == 0:
                    pe.wait_ge(probs_taken, KD)
                else:
                    pe.wait_ge(s_taken, rd)
                for u in range(4):
                    pe.transpose(pt[0][:, u * P:(u + 1) * P], probs_s[rd % 2][:, u, 0:WINDOW], ident)
                    tr = pe.transpose(pt[1][0:NQ, u * P:(u + 1) * P], probs_s[rd % 2][:, u, WINDOW:SKEYS], ident)
                tr.then_inc(s_turned, 1)
                if rd + 1 < NB // 2:
                    sample_scores(rd + 1, 1)
                pe.wait_ge(s_taken, rd + 1)
                if rd == 0:
                    pe.wait_ge(out_read, KD)
                else:
                    pe.wait_ge(s_out_read, 2 * rd)
                for u in range(4):
                    n, a = 2 * rd + u // 2, u % 2
                    for half in range(2):
                        rows = slice(HD * half, HD * half + HD)
                        head = slice((2 * a + half) * HD, (2 * a + half + 1) * HD)
                        cols = slice(u * P + HD * half, u * P + HD * half + HD)
                        pe.matmul(ot[rows, u * HD:(u + 1) * HD], v_c[:, n, head], probs_t[:, cols],
                                  start=True, stop=False)
                        mm = pe.matmul(ot[rows, u * HD:(u + 1) * HD], v_n[0:NQ, n, head], probs_tn[0:NQ, cols],
                                       start=False, stop=True)
                mm.then_inc(s_out_ready, 1)

            project_residual(ph["w_o"], xh, xl, 3, event=RHS_ATTN)
            ffn(1, RHS_MIX1)

        @block.scalar
        def _(act):
            def split_hi(p, ip, par_, wait=True, chunks=(0, 1)):
                for j in chunks:
                    slot, n = 2 * par_ + j, p.kt * P
                    act.wait_ge(raw_loaded[slot], 16 * bank_count(p, ip))
                    if wait:
                        act.wait_ge(multiplied, chunk(p, ip, par_, j) - 3)
                    act.copy(w_hi[:, slot, 0:n], w_raw[:, slot, 0:n]).then_inc(hi_ready, 1)

            def split_next(p, ip, par_, end, chunks=(0, 1)):
                if not end:
                    split_hi(p, ip + 1, par_, chunks=chunks)
                elif p.name in after:
                    split_hi(after[p.name], 0, par_, chunks=chunks)

            def pairs(p, body, first=0, side_by_side=False):
                n = p.groups // 2
                if side_by_side:
                    body(0, False, early=True)
                    first = 1
                with act.Fori(first, n - 1) as ip:
                    body(ip, False)
                body(n - 1, True)

            def square(n, k, src, dst):
                act.wait_ge(shifted, KD * n + k + 1)
                act.activation(dst, src, ACT.Square).then_inc(squared, 1)

            def norm(n, src, fn, g, b, l, nxt, rhs):
                act.wait_ge(mean_ready, n + 1)
                act.copy(shift, st[:, 0:T]).then_inc(mean_taken, 1)
                act.wait_ge(mean_taken, n + 1)
                act.activation(work[:, 0, :], shift, ACT.Square).then_inc(mean_squared, 1)
                act.wait_ge(var_ready, n + 1)
                act.activation(rstd, rstd, ACT.Sqrt, bias=const("eps")).then_inc(std_ready, 1)
                if nxt:
                    split_hi(nxt, 0, 1, chunks=(1,))
                for bt, (lo, hi) in enumerate(BATCHES):
                    act.wait_ge(scaled, NBT * n + bt + 1)
                    if rhs is None and bt == NBT - 1:
                        continue
                    for k in range(lo, hi):
                        act.activation(src[:, k, :], src[:, k, :], fn, bias=par(b)[:, k + KD * l, :],
                                       scale=par(g)[:, k + KD * l, :]).then_inc(applied, 1)
                    if rhs is not None:
                        act.wait_ge(applied, KD * n + hi)
                        act.copy(xh[:, lo:hi, :], src[:, lo:hi, :]).then_inc(rhs_hi_ready, 1)

            act.wait_ge(zero_ready, 2)
            act.copy(rstd[:, 0:1], shift[:, 0:1])
            split_hi(ph["w_in"], 0, 0, wait=False, chunks=(0,))
            for bt, (lo, hi) in enumerate(BATCHES):
                act.wait_ge(x_loaded[bt], 16)
                act.copy(xh[:, lo:hi, :], xr[:, lo:hi, :]).then_inc(rhs_hi_ready, 1)
                if bt == 0:
                    split_hi(ph["w_in"], 0, 1, wait=False, chunks=(0,))
                if bt == 3:
                    split_hi(ph["w_in"], 0, 0, wait=False, chunks=(1,))
                if bt == 4:
                    split_hi(ph["w_in"], 0, 1, wait=False, chunks=(1,))
            split_hi(ph["w_in"], 1, 0, chunks=(0,))
            act.activation(rstd[:, 0:1], shift[:, 0:1], ACT.Sigmoid)
            act.wait_ge(tables_loaded, 32)

            p = ph["w_in"]
            act.wait_ge(zero_ready, 1)

            def conv_square(i, first=False):
                if not first:
                    act.wait_ge(square_added, i)
                square(0, i, conv_y[:, i, :], work[:, 1, :])

            def glu(i, end, first=False):
                act.wait_ge(multiplied, group_done(p, i, 0))
                act.activation(work[:, 0, :], acc[0][:, 0:T], ACT.Sigmoid, bias=par("b_in")[:, i + KD, :]
                               ).then_inc(bank_read[0], 1)
                split_next(p, i, 0, end, chunks=(1,) if first else (0, 1))
                if not end:
                    split_next(p, i, 1, end)
                act.wait_ge(bank_read[1], bank_count(p, i))
                if not first:
                    act.wait_ge(dve_taps, DVE_TAPS * i)
                    act.wait_ge(prod_ready, POOL_TAPS * i)
                    act.wait_ge(state_saved, 16 * i)
                if isinstance(i, int):
                    act.wait_ge(hist_loaded, 16 if first else 32)
                windows = bass.AP(u_pad[:, :].tensor, 0, [u_pad[:, :].ap[0], [SEG, PSEG], [1, SEGW]])
                act.copy(u_seg[:, 0:PSEG, :], windows)
                act.copy(u_seg[:, PSEG:NSEG, 0:HIST], hist[:, i, :, :])
                act.copy(u_seg[:, PSEG:NSEG, HIST:SEGW],
                         u_pad[:, HIST + SEQ:HIST + T].rearrange("p (n q) -> p n q", q=NQ)).then_inc(useg_built, 1)
                act.wait_ge(useg_built, i + 1)
                act.dma_start(io["conv_state_out"][:, i], u_seg[:, PSEG - 1:NSEG, SEG:SEGW]).then_inc(state_saved, 16)
                for n in range(POOL_TAPS):
                    tap = DVE_TAPS + n
                    if not first:
                        act.wait_ge(pool_taps, POOL_TAPS * (i - 1) + n + 1)
                    act.activation(prods[:, n, :].rearrange("p (s q) -> p s q", q=SEG), u_seg[:, :, tap:tap + SEG],
                                   ACT.Identity, scale=par("w_dw")[:, i, tap:tap + 1]).then_inc(prod_ready, 1)
                if end:
                    split_next(p, i, 1, end, chunks=(0,))
                act.activation(xr[:, i, :], xr[:, i, :], ACT.Identity, bias=par("b_out")[:, i, :], scale=ALPHA)

            def glu_and_square(i, end):
                glu(i, end)
                conv_square(i - 1)

            act.wait_ge(rhs_ready, NBT)
            glu(0, False, first=True)
            glu(1, False)
            conv_square(0, first=True)
            pairs(p, glu_and_square, first=2)
            act.activation(rstd[:, 0:1], const("eps"), ACT.Sqrt)
            act.wait_ge(products_summed, POOL_TAPS)
            act.wait_ge(shifted, KD - 1)
            act.copy(taps_pool[:, :], pt[0][:, 0:T]).then_inc(sum_taken, 1)
            conv_square(KD - 1)
            norm(0, conv_y, ACT.Silu, "norm_g", "norm_b", 0, after[p.name], RHS_CONV)

            def weights_only(p):
                def body(ip, end):
                    for par_ in range(2):
                        split_next(p, ip, par_, end)
                pairs(p, body)

            def residual(p, n):
                split_hi(p, 1, 0)
                split_hi(p, 1, 1)
                square(n, 0, xr[:, 0, :], acc_sq)
                square(n, 1, xr[:, 1, :], work[:, 1, :])

                def body(ip, end):
                    split_next(p, ip, 0, end)
                    act.wait_ge(sq_added, (KD - 2) * (n - 1) + 2 * ip - 1)
                    square(n, 2 * ip, xr[:, 2 * ip, :], work[:, 1, :])
                    if not end:
                        split_next(p, ip, 1, end)
                    else:
                        if p.name in after:
                            split_hi(after[p.name], 0, 1, chunks=(0,))
                        act.activation(rstd[:, 0:1], const("eps"), ACT.Sqrt)
                        act.wait_ge(bank_read[1], bank_count(p, ip))
                    act.wait_ge(sq_added, (KD - 2) * (n - 1) + 2 * ip)
                    square(n, 2 * ip + 1, xr[:, 2 * ip + 1, :], work[:, 1, :])

                pairs(p, body, first=1)

            residual(ph["w_out"], 1)
            norm(1, xr, ACT.Identity, "mix_g", "mix_b", 0, after["w_out"], RHS_MIX0)

            def ffn(l):
                act.wait_ge(ffn_in_loaded, 16 * (l + 1))
                if l:
                    act.wait_ge(ffn_out_saved, 16 * l)
                    act.wait_ge(kv_saved, 64)
                else:
                    act.wait_ge(state_saved, 16 * KD)
                for h in range(2):
                    p = ph[f"up{l}{h}"]

                    def body(i, end, early=False):
                        if early:
                            split_next(p, i, 0, end, chunks=(0,))
                        f, tile = i + HALF * h, i + KF * l + HALF * h
                        taps = par("f_w_dw")[:, tile, :]
                        act.wait_ge(multiplied, group_done(p, i, 0))
                        gate = acc[0][:, 0:T].rearrange("p (s q) -> p s q", q=SEG)
                        act.activation(work[:, 0, :], acc[0][:, 0:T], ACT.Identity, bias=par("f_b_dw")[:, tile, :],
                                       scale=taps[:, 2:3])
                        act.copy(gate_s[:, :, FW - 1:FW - 1 + NQ], gate[:, PSEG:NSEG, :])
                        act.copy(gate_s[:, :, 0:FW - 1], ffn_in[:, f, :, :])
                        act.copy(ffn_out[:, f, :, :], gate[:, PSEG - 1:NSEG, SEG - (FW - 1):SEG]
                                 ).then_inc(gate_taken, 1)
                        split_next(p, i, 0, end, chunks=(1,) if early else (0, 1))
                        act.wait_ge(bank_read[0], bank_count(p, i))
                        act.activation(work[:, 0, :], work[:, 0, :], ACT.Gelu).then_inc(gelu_done, 1)
                        act.wait_ge(bank_read[1], bank_count(p, i))
                        act.copy(hh[:, i, :], work[:, 1, :]).then_inc(h_hi_ready, 1)
                        split_next(p, i, 1, end)

                    act.activation(rstd[:, 0:1], const("eps"), ACT.Gelu)
                    pairs(p, body, side_by_side=(h == 0))
                    if h == 0:
                        weights_only(ph[f"down{l}{h}"])
                    else:
                        residual(ph[f"down{l}{h}"], 2 * l + 2)

            ffn(0)
            norm(2, xr, ACT.Identity, "ffn_g", "ffn_b", 0, after["down01"], RHS_FFN0)
            weights_only(ph["w_kv"])

            p = ph["w_q"]

            def take_probs(pair, par_):
                t = 2 * pair + par_
                act.wait_ge(probs_turned, t + 1)
                act.copy(probs_t[:, 0:3 * P], pt[0][:, 0:3 * P])
                act.copy(probs_t[:, 3 * P:6 * P], pt[1][:, 0:3 * P]).then_inc(probs_taken, 1)

            def exponentials(pair, par_, a):
                t = 2 * pair + par_
                act.wait_ge(softmax_step, 10 * t + 4)
                for r in range(2):
                    act.activation(probs[:, r, 0, :], probs[:, r, 0, :], ACT.Exp, bias=negmax[:, 2 * r:2 * r + 1],
                                   accum_out=rowsum[:, 2 * r:2 * r + 1])
                    act.activation(probs[:, r, 1:3, :], probs[:, r, 1:3, :], ACT.Exp,
                                   bias=negmax[:, 2 * r + 1:2 * r + 2], accum_out=rowsum[:, 2 * r + 1:2 * r + 2])
                    ex = act.activation(sinkexp[:, 2 * r:2 * r + 2], negmax[:, 2 * r:2 * r + 2], ACT.Exp,
                                        bias=par("sinks")[:, 8 * a + 8 * r + t, :])
                ex.then_inc(exp_done, 1)

            def q_pair(ip, a1, a2, end=False):
                take_probs(ip - 1, 0)
                split_hi(p, ip, 1)
                exponentials(ip - 1, 1, a1)
                take_probs(ip - 1, 1)
                if not end:
                    split_hi(p, ip + 1, 0)
                else:
                    split_hi(after[p.name], 0, 0)
                exponentials(ip, 0, a2)

            act.wait_ge(v_transposed, 1)
            act.copy(v_p[:, :, :], pt[0][:, :].rearrange("p (b c) -> p b c", b=2))
            for n2, src in enumerate([sc[0], sc[1], pt[1], ot]):
                cp = act.copy(v_n[0:NQ, 2 * n2:2 * n2 + 2, :], src[0:NQ, :].rearrange("p (b c) -> p b c", b=2))
            cp.then_inc(v_taken, 1)
            split_hi(p, 1, 0)
            exponentials(0, 0, 0)
            with act.Fori(1, KD // 4) as ip:
                q_pair(ip, 0, 0)
            q_pair(KD // 4, 0, 1)
            with act.Fori(KD // 4 + 1, KD // 2 - 1) as ip:
                q_pair(ip, 1, 1)
            last = KD // 2 - 1
            q_pair(last, 1, 1, end=True)
            take_probs(last, 0)
            exponentials(last, 1, 1)
            take_probs(last, 1)

            act.wait_ge(kv_saved, 64)
            for rd in range(NB // 2):
                act.wait_ge(s_step, 9 * rd + 3)
                for u in range(4):
                    act.activation(probs_s[rd % 2][:, u, :], probs_s[rd % 2][:, u, :], ACT.Exp, bias=negmax[:, u:u + 1],
                                   accum_out=rowsum[:, u:u + 1])
                for a in range(2):
                    ex = act.activation(sinkexp[:, a:a + 3:2], negmax[:, a:a + 3:2], ACT.Exp,
                                        bias=par("sinks_s")[:, a, :])
                ex.then_inc(s_exp_done, 1)
                act.wait_ge(s_turned, rd + 1)
                if rd == 0:
                    act.wait_ge(out_ready, KD)
                else:
                    act.wait_ge(s_out_ready, rd)
                act.copy(probs_t[:, 0:4 * P], pt[0][:, :])
                act.copy(probs_tn[0:NQ, 0:4 * P], pt[1][0:NQ, :]).then_inc(s_taken, 1)
                if rd < 2:
                    split_hi(after[p.name], 0, 1, chunks=(rd,))

            act.wait_ge(s_out_read, NB)
            for lo, hi in BATCHES:
                act.copy(xh[:, lo:hi, :], qo[:, lo:hi, :]).then_inc(rhs_hi_ready, 1)
            residual(ph["w_o"], 3)
            norm(3, xr, ACT.Identity, "mix_g", "mix_b", 1, after["w_o"], RHS_MIX1)
            ffn(1)
            norm(4, xr, ACT.Identity, "ffn_g", "ffn_b", 1, None, None)

        @block.vector
        def _(dve):
            def split_lo(p, ip, par_, chunks=(0, 1)):
                for j in chunks:
                    slot, n = 2 * par_ + j, p.kt * P
                    dve.wait_ge(hi_ready, splits(p, ip, par_, j))
                    dve.tensor_tensor(w_lo[:, slot, 0:n], w_raw[:, slot, 0:n], w_hi[:, slot, 0:n],
                                      ALU.subtract).then_inc(lo_ready, 1)

            def split_next(p, ip, par_, end, chunks=(0, 1)):
                if not end:
                    split_lo(p, ip + 1, par_, chunks)
                elif p.name in after:
                    split_lo(after[p.name], 0, par_, chunks)

            def pairs(p, body, first=0, side_by_side=False):
                n = p.groups // 2
                if side_by_side:
                    body(0, False, early=True)
                    first = 1
                with dve.Fori(first, n - 1) as ip:
                    body(ip, False)
                body(n - 1, True)

            def rhs_lo(base, bt, src):
                lo, hi = BATCHES[bt]
                dve.wait_ge(rhs_hi_ready, base + bt + 1)
                dve.tensor_tensor(xl[:, lo:hi, :], src[:, lo:hi, :], xh[:, lo:hi, :], ALU.subtract
                                  ).then_inc(rhs_ready, 1)

            def norm(n, src, nxt, rhs):
                def center(bt):
                    lo, hi = BATCHES[bt]
                    dve.tensor_tensor(src[:, lo:hi, :], src[:, lo:hi, :], over_tiles(shift, hi - lo),
                                      ALU.subtract).then_inc(centered, 1)

                dve.wait_ge(mean_taken, n + 1)
                center(0)
                dve.wait_ge(moments_ready, n + 1)
                dve.wait_ge(mean_squared, n + 1)
                dve.tensor_tensor(rstd, ot[:, 0:T], work[:, 0, :], ALU.subtract).then_inc(var_ready, 1)
                center(1)
                dve.wait_ge(std_ready, n + 1)
                dve.reciprocal(rstd, rstd).then_inc(rstd_ready, 1)
                dve.wait_ge(rstd_ready, n + 1)

                def scale(bt):
                    lo, hi = BATCHES[bt]
                    if bt < VECTOR_CENTERS:
                        dve.wait_ge(centered, VECTOR_CENTERS * n + bt + 1)
                    else:
                        dve.wait_ge(pool_centered, (NBT - VECTOR_CENTERS) * n + bt - VECTOR_CENTERS + 1)
                    dve.tensor_tensor(src[:, lo:hi, :], src[:, lo:hi, :], over_tiles(rstd, hi - lo),
                                      ALU.mult).then_inc(scaled, 1)

                def lo_part(bt):
                    if rhs is not None:
                        rhs_lo(rhs, bt, src)

                scale(0)
                center(2)
                scale(1)
                lo_part(0)
                scale(2)
                lo_part(1)
                for bt in range(3, NBT):
                    scale(bt)
                    if bt == 4 and nxt:
                        split_lo(nxt, 0, 1, chunks=(1,))
                    lo_part(bt - 1)
                lo_part(NBT - 1)
                if rhs is None:
                    lo, hi = BATCHES[-1]
                    dve.wait_ge(scaled, NBT * (n + 1))
                    for k in range(lo, hi):
                        at = k + KD * (LAYERS - 1)
                        dve.tensor_scalar(src[:, k, :], src[:, k, :], par("ffn_g")[:, at, :], par("ffn_b")[:, at, :],
                                          ALU.mult, ALU.add).then_inc(last_applied, 1)

            dve.memset(u_pad[:, 0:HIST], 0.0).then_inc(zero_ready, 1)
            dve.memset(shift, 0.0).then_inc(zero_ready, 1)
            split_lo(ph["w_in"], 0, 0, chunks=(0,))
            for bt in range(NBT):
                rhs_lo(RHS_X, bt, xr)
                if bt == 0:
                    split_lo(ph["w_in"], 0, 1, chunks=(0,))
                if bt == 3:
                    split_lo(ph["w_in"], 0, 0, chunks=(1,))
                if bt == 4:
                    split_lo(ph["w_in"], 0, 1, chunks=(1,))
            split_lo(ph["w_in"], 1, 0, chunks=(0,))
            dve.wait_ge(tables_loaded, 32)

            p = ph["w_in"]

            def gate(i):
                dve.wait_ge(bank_read[0], bank_count(p, i))
                dve.wait_ge(multiplied, group_done(p, i, 1))
                dve.scalar_tensor_tensor(u_pad[:, HIST:HIST + T], acc[1][:, 0:T], par("b_in")[:, i, :], work[:, 0, :],
                                         ALU.add, ALU.mult).then_inc(bank_read[1], 1)

            def conv_taps(i, first=False):
                dve.wait_ge(useg_built, i + 1)
                sums = [b[:, 0:T].rearrange("p (s q) -> p s q", q=SEG) for b in sc]
                w = par("w_dw")[:, i, :]
                steps = DVE_TAPS * i
                dve.tensor_scalar(sums[0], u_seg[:, :, 0:SEG], w[:, 0:1], par("b_dw")[:, i, :], ALU.mult, ALU.add
                                  ).then_inc(dve_taps, 1)
                if not first:
                    dve.wait_ge(shifted, i)
                dve.tensor_scalar(sums[1], u_seg[:, :, 1:1 + SEG], w[:, 1:2], None, ALU.mult).then_inc(dve_taps, 1)
                for tap in range(2, DVE_TAPS):
                    dst = sums[tap % 2]
                    dve.wait_ge(dve_taps, steps + tap - 1)
                    dve.scalar_tensor_tensor(dst, u_seg[:, :, tap:tap + SEG], w[:, tap:tap + 1], dst,
                                             ALU.mult, ALU.add).then_inc(dve_taps, 1)

            def conv(i, end):
                split_next(p, i, 0, end)
                gate(i)
                if not end:
                    split_next(p, i, 1, end)
                join(i - 1)
                conv_taps(i)

            def join(i, done=shifted):
                dve.wait_ge(dve_taps, DVE_TAPS * (i + 1))
                if isinstance(i, int) and i == KD - 1:
                    dve.wait_ge(sum_taken, 1)
                else:
                    dve.wait_ge(pool_taps, POOL_TAPS * (i + 1))
                dve.tensor_tensor(taps_pool[:, :], sc[0][:, 0:T], taps_pool[:, :], ALU.add).then_inc(parts_joined, 1)
                dve.wait_ge(parts_joined, i + 1)
                dve.tensor_tensor(conv_y[:, i, :], sc[1][:, 0:T], taps_pool[:, :], ALU.add).then_inc(done, 1)

            split_next(p, 0, 0, False, chunks=(1,))
            gate(0)
            split_next(p, 0, 1, False)
            conv_taps(0, first=True)
            split_next(p, 1, 0, False)
            gate(1)
            join(0, conv0_done)
            split_next(p, 1, 1, False)
            dve.wait_ge(shift_ready, 1)
            dve.tensor_scalar(shift, pt[0][:, 0:T], -1.0, None, ALU.mult).then_inc(shift_taken, 1)
            dve.wait_ge(shift_taken, 1)
            dve.tensor_tensor(conv_y[:, 0, :], conv_y[:, 0, :], shift, ALU.add).then_inc(shifted, 1)
            conv_taps(1)
            pairs(p, conv, first=2)
            join(KD - 1)
            split_next(p, KD - 1, 1, True, chunks=(0,))
            norm(0, conv_y, after[p.name], RHS_CONV)

            def add_projection(p, ip, par_, scale):
                k = 2 * ip + par_
                dve.wait_ge(multiplied, group_done(p, ip, par_))
                dve.scalar_tensor_tensor(xr[:, k, :], xr[:, k, :], scale, acc[par_][:, 0:T],
                                         ALU.mult, ALU.add).then_inc(bank_read[par_], 1)

            def residual(p, scale, n, side_by_side=True):
                if side_by_side:
                    split_next(p, 0, 0, False, chunks=(0,))
                add_projection(p, 0, 0, scale)
                split_next(p, 0, 0, False, chunks=(1,) if side_by_side else (0, 1))
                add_projection(p, 0, 1, scale)
                split_next(p, 0, 1, False)
                dve.wait_ge(shift_ready, n + 1)
                dve.tensor_copy(shift, st[:, 0:T]).then_inc(shift_taken, 1)
                dve.wait_ge(shift_taken, n + 1)
                dve.tensor_tensor(xr[:, 0:2, :], xr[:, 0:2, :], over_tiles(shift, 2), ALU.subtract
                                  ).then_inc(shifted, 2)
                dve.wait_ge(shifted, KD * n + 2)
                dve.tensor_tensor(acc_sum, xr[:, 0, :], xr[:, 1, :], ALU.add).then_inc(sum_added, 1)
                dve.wait_ge(squared, KD * n + 2)
                dve.tensor_tensor(acc_sq, acc_sq, work[:, 1, :], ALU.add).then_inc(sq_added, 1)

                def body(ip, end):
                    for par_ in range(2):
                        k = 2 * ip + par_
                        if end and par_ == 1:
                            dve.scalar_tensor_tensor(xr[:, k, :], xr[:, k, :], scale, shift, ALU.mult, ALU.subtract
                                                     ).then_inc(shifted, 1)
                            if p.name in after:
                                split_lo(after[p.name], 0, 1, chunks=(0,))
                            dve.wait_ge(multiplied, group_done(p, ip, par_))
                            dve.wait_ge(shifted, KD * (n + 1))
                            dve.tensor_tensor(xr[:, k, :], xr[:, k, :], acc[par_][:, 0:T], ALU.add
                                              ).then_inc(bank_read[par_], 1)
                            break
                        add_projection(p, ip, par_, scale)
                        dve.wait_ge(bank_read[par_], bank_count(p, ip))
                        dve.tensor_tensor(xr[:, k, :], xr[:, k, :], shift, ALU.subtract).then_inc(shifted, 1)
                        split_next(p, ip, par_, end, chunks=(0,) if end else (0, 1))
                        dve.wait_ge(shifted, KD * n + k + 1)
                        dve.wait_ge(sum_added, (KD - 2) * (n - 1) + k - 1)
                        dve.tensor_tensor(acc_sum, acc_sum, xr[:, k, :], ALU.add).then_inc(sum_added, 1)
                        dve.wait_ge(squared, KD * n + k + 1)
                        dve.wait_ge(sq_added, (KD - 2) * (n - 1) + k - 1)
                        dve.tensor_tensor(acc_sq, acc_sq, work[:, 1, :], ALU.add).then_inc(sq_added, 1)
                        if end:
                            split_next(p, ip, par_, end, chunks=(1,))

                pairs(p, body, first=1)

            def residual_only(p, scale):
                def body(ip, end):
                    for par_ in range(2):
                        add_projection(p, ip, par_, scale)
                        split_next(p, ip, par_, end)
                pairs(p, body)

            residual(ph["w_out"], 1.0, 1)
            norm(1, xr, after["w_out"], RHS_MIX0)

            def ffn(l, n_norm, rhs):
                if l:
                    dve.wait_ge(kv_saved, 64)
                else:
                    dve.wait_ge(state_saved, 16 * KD)
                for h in range(2):
                    p = ph[f"up{l}{h}"]

                    def body(i, end, early=False):
                        if early:
                            split_next(p, i, 0, end, chunks=(0,))
                        tile = i + KF * l + HALF * h
                        taps = par("f_w_dw")[:, tile, :]
                        gy = work[:, 0, :]
                        gy_s = work[:, 0, SEQ:T].rearrange("p (n q) -> p n q", q=NQ)
                        dve.wait_ge(gate_taken, tile + 1)
                        dve.scalar_tensor_tensor(gy[:, 1:SEQ], acc[0][:, 0:SEQ - 1], taps[:, 1:2], gy[:, 1:SEQ],
                                                 ALU.mult, ALU.add).then_inc(taps_done, 1)
                        dve.scalar_tensor_tensor(gy_s, gate_s[:, :, 1:1 + NQ], taps[:, 1:2], gy_s,
                                                 ALU.mult, ALU.add).then_inc(taps_done, 1)
                        dve.wait_ge(taps_done, 3 * tile + 1)
                        dve.scalar_tensor_tensor(gy[:, 2:SEQ], acc[0][:, 0:SEQ - 2], taps[:, 0:1], gy[:, 2:SEQ],
                                                 ALU.mult, ALU.add).then_inc(taps_done, 1)
                        dve.wait_ge(taps_done, 3 * tile + 2)
                        dve.scalar_tensor_tensor(gy_s, gate_s[:, :, 0:NQ], taps[:, 0:1], gy_s,
                                                 ALU.mult, ALU.add).then_inc(bank_read[0], 1)
                        split_next(p, i, 0, end, chunks=(1,) if early else (0, 1))
                        dve.wait_ge(multiplied, group_done(p, i, 1))
                        dve.wait_ge(gelu_done, tile + 1)
                        dve.tensor_tensor(work[:, 1, :], gy, acc[1][:, 0:T], ALU.mult).then_inc(bank_read[1], 1)
                        split_next(p, i, 1, end)
                        dve.wait_ge(h_hi_ready, tile + 1)
                        dve.tensor_tensor(hl[:, i, :], work[:, 1, :], hh[:, i, :], ALU.subtract).then_inc(h_ready, 1)

                    pairs(p, body, side_by_side=(h == 0))
                    down = ph[f"down{l}{h}"]
                    if h == 0:
                        residual_only(down, ALPHA)
                    else:
                        residual(down, 1.0, n_norm, side_by_side=False)
                norm(n_norm, xr, after.get(down.name), rhs)

            ffn(0, 2, RHS_FFN0)

            p = ph["w_kv"]
            split_next(p, 0, 0, False, chunks=(0,))
            for ip, dst in enumerate([k_t, v_t]):
                for par_ in range(2):
                    dve.wait_ge(multiplied, group_done(p, ip, par_))
                    dve.tensor_copy(dst[:, par_, :], acc[par_][:, 0:T]).then_inc(bank_read[par_], 1)
                    split_next(p, ip, par_, ip == 1, chunks=(1,) if (ip, par_) == (0, 0) else (0, 1))

            p = ph["w_q"]

            def softmax_max(pair, par_, a):
                t = 2 * pair + par_
                if not (isinstance(t, int) and t == 0):
                    dve.wait_ge(probs_turned, t)
                dist = const("dist").rearrange("p a b -> p (a b)")
                for r in range(2):
                    dve.wait_ge(scores_ready, 2 * t + r + 1)
                    dve.scalar_tensor_tensor(probs[:, r, :, :].rearrange("p a b -> p (a b)"), dist,
                                             const("negslope")[:, 8 * a + 8 * r + t, :], sc[r][:, 0:3 * P],
                                             ALU.mult, ALU.add).then_inc(scores_read, 1)
                dve.wait_ge(scores_read, 2 * t + 2)
                dve.tensor_reduce(rowmax, probs[:, :, :, :].rearrange("p a b c -> p (a b) c"), AXX, ALU.max
                                  ).then_inc(softmax_step, 1)
                dve.wait_ge(softmax_step, 10 * t + 1)
                rm = rowmax.rearrange("p (r c) -> p r c", c=3)
                dve.tensor_tensor(rm[:, :, 1:2], rm[:, :, 1:2], rm[:, :, 2:3], ALU.max).then_inc(softmax_step, 1)
                dve.wait_ge(softmax_step, 10 * t + 2)
                for r in range(2):
                    dve.tensor_scalar(negmax[:, 2 * r:2 * r + 2], rm[:, r, 0:2], par("sinks")[:, 8 * a + 8 * r + t, :],
                                      -1.0, ALU.max, ALU.mult).then_inc(softmax_step, 1)

            def softmax_divide(pair, par_):
                t = 2 * pair + par_
                dve.wait_ge(exp_done, t + 1)
                dve.tensor_tensor(denom, rowsum, sinkexp, ALU.add).then_inc(softmax_step, 1)
                dve.wait_ge(softmax_step, 10 * t + 5)
                dve.reciprocal(rdenom, denom).then_inc(softmax_step, 1)
                dve.wait_ge(softmax_step, 10 * t + 6)
                for r in range(2):
                    dve.tensor_scalar(probs[:, r, 0, :], probs[:, r, 0, :], rdenom[:, 2 * r:2 * r + 1], None,
                                      ALU.mult).then_inc(softmax_step, 1)
                    dve.tensor_scalar(probs[:, r, 1:3, :], probs[:, r, 1:3, :], rdenom[:, 2 * r + 1:2 * r + 2], None,
                                      ALU.mult).then_inc(softmax_step, 1)

            def take_out(pair, par_):
                t = 2 * pair + par_
                dve.wait_ge(out_ready, t + 1)
                dve.tensor_copy(qo[:, t, 0:SEQ], ot[:, 0:SEQ]).then_inc(out_read, 1)

            def take_q(ip, par_, a):
                dve.wait_ge(multiplied, group_done(p, ip, par_))
                dve.tensor_scalar(q_st[:, par_, :], acc[par_][:, 0:SEQ], QSCALE, None, ALU.mult)
                dve.tensor_scalar(q_s[:, a, :, 2 * ip + par_ - 8 * a, :],
                                  acc[par_][:, SEQ:T].rearrange("p (n q) -> p n q", q=NQ), QSCALE, None, ALU.mult
                                  ).then_inc(bank_read[par_], 1)

            def q_pair(ip, a1, a2, end=False):
                softmax_max(ip - 1, 1, a1)
                split_lo(p, ip, 1)
                softmax_divide(ip - 1, 1)
                take_out(ip - 1, 0)
                take_q(ip, 0, a2)
                softmax_max(ip, 0, a2)
                if not end:
                    split_lo(p, ip + 1, 0)
                else:
                    split_lo(after[p.name], 0, 0)
                softmax_divide(ip, 0)
                take_out(ip - 1, 1)
                take_q(ip, 1, a2)

            take_q(0, 0, 0)
            softmax_max(0, 0, 0)
            split_lo(p, 1, 0)
            softmax_divide(0, 0)
            take_q(0, 1, 0)
            with dve.Fori(1, KD // 4) as ip:
                q_pair(ip, 0, 0)
            q_pair(KD // 4, 0, 1)
            with dve.Fori(KD // 4 + 1, KD // 2 - 1) as ip:
                q_pair(ip, 1, 1)
            last = KD // 2 - 1
            q_pair(last, 1, 1, end=True)
            softmax_max(last, 1, 1)
            softmax_divide(last, 1)
            take_out(last, 0)

            def take_sample_out(rd):
                dve.wait_ge(s_out_ready, rd + 1)
                for x in range(2):
                    n = 2 * rd + x
                    dve.tensor_copy(qo[:, :, SEQ + n * NQ:SEQ + (n + 1) * NQ],
                                    ot[:, x * P:(x + 1) * P].rearrange("p (t q) -> p t q", q=NQ)
                                    ).then_inc(s_out_read, 1)

            for rd in range(NB // 2):
                pr = probs_s[rd % 2]
                if rd == 0:
                    dve.wait_ge(probs_turned, KD)
                elif rd == 1:
                    dve.wait_ge(ffn_out_saved, 16)
                else:
                    dve.wait_ge(s_turned, rd - 1)
                for u in range(4):
                    dve.wait_ge(s_scores_ready, 2 * rd + u // 2 + 1)
                    a = u % 2
                    dve.scalar_tensor_tensor(pr[:, u, :], const("dist_s"), const("negslope_s")[:, a, :],
                                             sc[u // 2][:, a * SKEYS:(a + 1) * SKEYS], ALU.mult, ALU.add
                                             ).then_inc(s_scores_read, 1)
                dve.wait_ge(s_scores_read, 4 * rd + 4)
                dve.tensor_reduce(rowmax[:, 0:4], pr, AXX, ALU.max).then_inc(s_step, 1)
                dve.wait_ge(s_step, 9 * rd + 1)
                for a in range(2):
                    dve.tensor_scalar(negmax[:, a:a + 3:2], rowmax[:, a:a + 3:2], par("sinks_s")[:, a, :], -1.0,
                                      ALU.max, ALU.mult).then_inc(s_step, 1)
                if rd == 0:
                    take_out(last, 1)
                else:
                    take_sample_out(rd - 1)
                dve.wait_ge(s_exp_done, rd + 1)
                dve.tensor_tensor(denom, rowsum, sinkexp, ALU.add).then_inc(s_step, 1)
                dve.wait_ge(s_step, 9 * rd + 4)
                dve.reciprocal(rdenom, denom).then_inc(s_step, 1)
                dve.wait_ge(s_step, 9 * rd + 5)
                for u in range(4):
                    dve.tensor_scalar(pr[:, u, :], pr[:, u, :], rdenom[:, u:u + 1], None, ALU.mult
                                      ).then_inc(s_step, 1)
                if rd in (1, 2):
                    split_lo(after[p.name], 0, 1, chunks=(rd - 1,))
            take_sample_out(NB // 2 - 1)

            for bt in range(NBT):
                rhs_lo(RHS_ATTN, bt, qo)
            residual(ph["w_o"], ALPHA, 3)
            norm(3, xr, after["w_o"], RHS_MIX1)
            ffn(1, 4, None)



_OUT = {
    "y": (P, KD, T),
    "conv_state_out": (P, KD, NB + 1, HIST),
    "ffn_state_out": (LAYERS, P, KF, NB + 1, FW - 1),
    "k_new": (P, 2, T),
    "v_new": (P, 2, T),
    "kc_out": (NB, WINDOW - NQ, 4 * HD),
    "vc_out": (NB, WINDOW - NQ, 4 * HD),
}


def _stream(w):
    k, n = w.shape
    return w.reshape(k // P, P, n // P, P).transpose(2, 1, 0, 3).reshape(n // P, P, k)


def _feature_tiles(v):
    v = v.reshape(v.shape[:-1] + (v.shape[-1] // P, P))
    return np.moveaxis(np.moveaxis(v, -1, 0), -1, 1)


def _pack(table, values):
    cols = []
    for name, shape in table:
        v = np.asarray(values[name], np.float32)
        cols.append(np.broadcast_to(v, (P,) + v.shape[1:]).reshape(P, -1))
    return np.concatenate(cols, axis=1)


def _constants():
    row = np.arange(P, dtype=np.float32)[:, None]
    col = np.arange(P, dtype=np.float32)[None, :]
    own = np.where(row >= col, row - col, MASKED)
    before = np.where(col >= row, WINDOW + row - col, MASKED)
    q = (np.arange(P) % NQ).astype(np.float32)[:, None]
    key = np.arange(SKEYS, dtype=np.float32)[None, :]
    d = WINDOW + q - key
    slopes = np.float32(2.0) ** (np.float32(-8.0) * np.arange(1, NH + 1, dtype=np.float32) / np.float32(NH))
    return {
        "ident": np.eye(P), "ones_mean": np.full((P, P), 1.0 / D),
        "ones_tile": np.full((P, P), 1.0 / P), "dist": np.stack([own, before, own], axis=1),
        "dist_s": np.where((d >= 0) & (d <= WINDOW), d, MASKED),
        "eps": np.full((P, 1), EPS), "negslope": -slopes[None, :, None],
        "negslope_s": -np.repeat(slopes.reshape(2, 2 * 8), NQ, axis=1).T[:, :, None],
    }


def kernel(**inputs):
    import concourse.bacc as _bacc
    from concourse.bass_utils import run_bass_kernel_spmd as _run

    a = {k: np.asarray(v) for k, v in inputs.items()}
    tokens = np.concatenate([a["x_prompt"].reshape(SEQ, D), a["x_sample"].reshape(NS, D)])
    wq = a["b_w_q"][0].reshape(D, 2, 2, 8, HD).transpose(0, 1, 3, 2, 4).reshape(D, D)
    wo = a["b_w_o"][0].reshape(2, 2, 8, HD, D).transpose(0, 2, 1, 3, 4).reshape(D, D)

    arrays = {"x": _feature_tiles(tokens.T[None].transpose(0, 2, 1))[:, :, 0]}
    w_in = _stream(a["a_w_in"][0])
    arrays["w_in"] = w_in.reshape(2, KD, P, D)[::-1].transpose(1, 0, 2, 3).reshape(2 * KD, P, D)
    arrays["w_out"] = _stream(a["a_w_out"][0])
    arrays["w_kv"], arrays["w_q"], arrays["w_o"] = _stream(a["w_kv"]), _stream(wq), _stream(wo)
    for l in range(LAYERS):
        up = _stream(a["f_w_up"][l]).reshape(2, KF, P, D)
        for h in range(2):
            part = slice(h * HALF, (h + 1) * HALF)
            arrays[f"up{l}{h}"] = up[:, part].transpose(1, 0, 2, 3).reshape(2 * HALF, P, D)
            arrays[f"down{l}{h}"] = _stream(a["f_w_down"][l][h * HALF * P:(h + 1) * HALF * P])
    arrays["conv_state"] = _feature_tiles(a["state_conv_a"][0])
    arrays["ffn_state"] = np.stack([_feature_tiles(s) for s in a["state_ffn_conv"]])
    kc = a["cache_k_win"].reshape(NB, WINDOW, 2, P)
    arrays["k_cache_t"] = kc.transpose(3, 2, 0, 1)
    arrays["k_cache"] = a["cache_k_win"].reshape(NB, WINDOW, 4 * HD)
    arrays["v_cache"] = a["cache_v_win"].reshape(NB, WINDOW, 4 * HD)

    def per_layer(v):
        v = np.stack([_feature_tiles(x) for x in v], axis=1)
        return v.reshape(P, -1, 1)

    sinks = a["b_sinks"][0]
    arrays["params"] = _pack(PARAMS, {
        "b_in": _feature_tiles(a["a_b_in"][0])[:, :, None], "w_dw": _feature_tiles(a["a_w_dw"][0]),
        "b_dw": _feature_tiles(a["a_b_dw"][0])[:, :, None], "norm_g": _feature_tiles(a["a_norm_g"][0])[:, :, None],
        "norm_b": _feature_tiles(a["a_norm_b"][0])[:, :, None], "b_out": _feature_tiles(a["a_b_out"][0])[:, :, None],
        "f_w_dw": np.concatenate([_feature_tiles(x) for x in a["f_w_dw"]], axis=1),
        "f_b_dw": per_layer(a["f_b_dw"]), "mix_g": per_layer(a["ln_mix_g"]), "mix_b": per_layer(a["ln_mix_b"]),
        "ffn_g": per_layer(a["ln_ffn_g"]), "ffn_b": per_layer(a["ln_ffn_b"]),
        "sinks": sinks[None, :, None],
        "sinks_s": np.repeat(sinks.reshape(2, 2 * 8), NQ, axis=1).T[:, :, None],
    })
    arrays["consts"] = _pack(CONSTS, _constants())

    nc = _bacc.Bacc("TRN2", target_bir_lowering=False, num_devices=1)
    io, feed = {}, {}
    for name, v in arrays.items():
        v = np.ascontiguousarray(v)
        feed[f"in_{name}"] = v
        io[name] = nc.dram_tensor(f"in_{name}", v.shape, F32, kind="ExternalInput").ap()
    for name, shape in _OUT.items():
        io[name] = nc.dram_tensor(f"out_{name}", shape, F32, kind="ExternalOutput").ap()
    trunk_kernel(nc, io)
    got = _run(nc, [feed], core_ids=[0]).results[0]
    o = {name: got[f"out_{name}"] for name in _OUT}

    def tokens_of(v):
        v = np.moveaxis(np.moveaxis(v, 1, -1), 0, -1)
        return v.reshape(v.shape[:-2] + (-1,))

    y = tokens_of(o["y"])
    conv = tokens_of(o["conv_state_out"])
    ffn = np.stack([tokens_of(v) for v in o["ffn_state_out"]])
    new = [tokens_of(o["k_new"]), tokens_of(o["v_new"])]
    win_p = [v[SEQ - WINDOW:SEQ].reshape(1, WINDOW, 4, HD) for v in new]
    win_s = [np.concatenate([old, v[SEQ:].reshape(NB, NQ, 4 * HD)], axis=1).reshape(NB, WINDOW, 4, HD)
             for old, v in zip([o["kc_out"], o["vc_out"]], new)]
    return (y[:SEQ].reshape(1, SEQ, D), y[SEQ:].reshape(NB, NQ, D), conv[None, 0:1], ffn[:, 0:1],
            win_p[0], win_p[1], conv[None, 1:], ffn[:, 1:], win_s[0], win_s[1])
```
